# Optimizing a Trainium2 kernel written in Bass

```python
import jax, jax.numpy as jnp
from jax import lax
import numpy as np

D_MODEL = 1024
BATCH = 1
SEQ = 1024
DEPTH = 2

GRID_W = 64
HEAD_DIM = 64
N_HEADS_A = D_MODEL // (2 * HEAD_DIM)
N_HEADS_B = D_MODEL // (4 * HEAD_DIM)
N_GROUPS_C = D_MODEL // (4 * HEAD_DIM)
WIDTH_A = N_HEADS_A * HEAD_DIM
WIDTH_B = N_HEADS_B * HEAD_DIM
WIDTH_C = N_GROUPS_C * HEAD_DIM
MIX_WIDTH = WIDTH_A + WIDTH_B + WIDTH_C
N_HEADS_TOTAL = MIX_WIDTH // HEAD_DIM
IN_WIDTH = 3 * WIDTH_A + 2 * WIDTH_B + WIDTH_C
NA_ROWS_MAX = 8
NA_COLS = 16
CHUNK = 128
D_FF = -(-8 * D_MODEL // (3 * 256)) * 256
EPS = 1e-6
NEG_INF = -1e9

kernel_name = "hybrid_natten_gmlp_fnet_encoder"

def rms_norm(x, g):
    xf = x.astype(jnp.float32)
    y = xf * lax.rsqrt(jnp.mean(xf * xf, axis=-1, keepdims=True) + EPS)
    return (y * g.astype(jnp.float32)).astype(x.dtype)

def layer_norm(x, g, b):
    xf = x.astype(jnp.float32)
    mu = jnp.mean(xf, axis=-1, keepdims=True)
    var = jnp.mean(jnp.square(xf - mu), axis=-1, keepdims=True)
    y = (xf - mu) * lax.rsqrt(var + EPS)
    return (y * g.astype(jnp.float32) + b.astype(jnp.float32)).astype(x.dtype)

def head_rms_norm(y, g):
    b_, s, _ = y.shape
    yf = y.astype(jnp.float32).reshape(b_, s, N_HEADS_TOTAL, HEAD_DIM)
    yf = yf * lax.rsqrt(jnp.mean(yf * yf, axis=-1, keepdims=True) + EPS)
    return (yf.reshape(b_, s, MIX_WIDTH) * g.astype(jnp.float32)).astype(y.dtype)

def neighbourhood_attention(q, k, v, rpb):
    b_, s, h, dh = q.shape
    rows = s // GRID_W
    kh = min(NA_ROWS_MAX, rows)
    kw = NA_COLS
    band = 2 * kw
    nqb = GRID_W // kw
    scale = HEAD_DIM ** -0.5

    qg = q.reshape(b_, rows, nqb, kw, h, dh)
    kg = k.reshape(b_, rows, GRID_W, h, dh)
    vg = v.reshape(b_, rows, GRID_W, h, dh)

    qcol = np.arange(GRID_W).reshape(nqb, kw)
    band_start = np.clip(np.arange(nqb) * kw - kw // 2, 0, GRID_W - band)
    band_cols = band_start[:, None] + np.arange(band)[None, :]
    win_start = np.clip(qcol - kw // 2, 0, GRID_W - kw)
    kc = band_cols[:, None, :]
    in_win = (kc >= win_start[..., None]) & (kc < win_start[..., None] + kw)
    dcol_idx = np.clip(kc - qcol[..., None] + NA_COLS - 1, 0, 2 * NA_COLS - 2)
    col_bias = rpb.astype(jnp.float32)[:, :, dcol_idx]
    col_bias = jnp.where(jnp.asarray(in_win)[None, None], col_bias, NEG_INF)

    def row_step(r):
        rs = jnp.clip(r - kh // 2, 0, rows - kh)
        k_slab = lax.dynamic_slice_in_dim(kg, rs, kh, axis=1)
        v_slab = lax.dynamic_slice_in_dim(vg, rs, kh, axis=1)
        k_band = k_slab[:, :, band_cols]
        v_band = v_slab[:, :, band_cols]
        q_row = lax.dynamic_index_in_dim(qg, r, axis=1, keepdims=False)
        sc = jnp.einsum('bjqhd,bkjnhd->bhjqkn', q_row, k_band).astype(jnp.float32) * scale
        drow_idx = rs + jnp.arange(kh) - r + NA_ROWS_MAX - 1
        bias = col_bias[:, drow_idx].transpose(0, 2, 3, 1, 4)
        logits = (sc + bias[None]).reshape(b_, h, nqb, kw, kh * band)
        p = jax.nn.softmax(logits, axis=-1).reshape(b_, h, nqb, kw, kh, band).astype(v.dtype)
        o = jnp.einsum('bhjqkn,bkjnhd->bjqhd', p, v_band)
        return o.reshape(b_, GRID_W, h, dh)

    out = lax.map(row_step, jnp.arange(rows))
    return out.transpose(1, 0, 2, 3, 4).reshape(b_, s, h * dh)

def spatial_gating(z, ln_g, ln_b, w_s, b_s):
    b_, s, _ = z.shape
    z = jax.nn.gelu(z)
    u, v = jnp.split(z, 2, axis=-1)
    v = layer_norm(v, ln_g, ln_b)
    vc = v.reshape(b_, s // CHUNK, CHUNK, N_HEADS_B, HEAD_DIM)
    mixed = jnp.einsum('hpq,bnqhd->bnphd', w_s, vc) + b_s.T[None, None, :, :, None]
    return u * mixed.reshape(b_, s, WIDTH_B)

def fourier_mix(xc):
    b_, s, _ = xc.shape
    xf = xc.astype(jnp.float32).reshape(b_, s, N_GROUPS_C, HEAD_DIM)
    y = jnp.real(jnp.fft.fft2(xf, axes=(1, 3), norm="ortho"))
    return y.astype(xc.dtype).reshape(b_, s, WIDTH_C)

def setup_inputs(seed: int = 0) -> dict:
    key = jax.random.key(seed)
    ks = jax.random.split(key, 16)
    f32 = jnp.float32
    nrm = lambda k, shp, sc: jax.random.normal(k, shp, f32) * sc
    return {
        "x": jax.random.normal(ks[0], (BATCH, SEQ, D_MODEL), f32),
        "norm_mix_g": 1.0 + nrm(ks[1], (DEPTH, D_MODEL), 0.05),
        "w_in": nrm(ks[2], (DEPTH, D_MODEL, IN_WIDTH), D_MODEL ** -0.5),
        "rpb": nrm(ks[3], (DEPTH, N_HEADS_A, 2 * NA_ROWS_MAX - 1, 2 * NA_COLS - 1), 0.5),
        "gmlp_ln_g": 1.0 + nrm(ks[4], (DEPTH, WIDTH_B), 0.05),
        "gmlp_ln_b": nrm(ks[5], (DEPTH, WIDTH_B), 0.02),
        "w_spatial": nrm(ks[6], (DEPTH, N_HEADS_B, CHUNK, CHUNK), CHUNK ** -0.5),
        "b_spatial": 1.0 + nrm(ks[7], (DEPTH, N_HEADS_B, CHUNK), 0.1),
        "head_norm_g": 1.0 + nrm(ks[8], (DEPTH, MIX_WIDTH), 0.05),
        "w_out": nrm(ks[9], (DEPTH, MIX_WIDTH, D_MODEL), MIX_WIDTH ** -0.5),
        "norm_ffn_g": 1.0 + nrm(ks[10], (DEPTH, D_MODEL), 0.05),
        "w_gate": nrm(ks[11], (DEPTH, D_MODEL, D_FF), D_MODEL ** -0.5),
        "w_up": nrm(ks[12], (DEPTH, D_MODEL, D_FF), D_MODEL ** -0.5),
        "w_down": nrm(ks[13], (DEPTH, D_FF, D_MODEL), D_FF ** -0.5),
        "final_norm_g": 1.0 + nrm(ks[14], (D_MODEL,), 0.05),
    }

def reference(x, norm_mix_g, w_in, rpb, gmlp_ln_g, gmlp_ln_b, w_spatial, b_spatial,
              head_norm_g, w_out, norm_ffn_g, w_gate, w_up, w_down, final_norm_g):
    b_, s, _ = x.shape
    splits = [WIDTH_A, 2 * WIDTH_A, 3 * WIDTH_A, 3 * WIDTH_A + 2 * WIDTH_B]
    for l in range(DEPTH):
        h = rms_norm(x, norm_mix_g[l])
        proj = h @ w_in[l]
        q, k, v, z_b, x_c = jnp.split(proj, splits, axis=-1)
        mix_a = neighbourhood_attention(q.reshape(b_, s, N_HEADS_A, HEAD_DIM),
                                        k.reshape(b_, s, N_HEADS_A, HEAD_DIM),
                                        v.reshape(b_, s, N_HEADS_A, HEAD_DIM), rpb[l])
        mix_b = spatial_gating(z_b, gmlp_ln_g[l], gmlp_ln_b[l], w_spatial[l], b_spatial[l])
        mix_c = fourier_mix(x_c)
        mix = head_rms_norm(jnp.concatenate([mix_a, mix_b, mix_c], axis=-1), head_norm_g[l])
        x = x + mix @ w_out[l]
        h = rms_norm(x, norm_ffn_g[l])
        x = x + (jax.nn.silu(h @ w_gate[l]) * (h @ w_up[l])) @ w_down[l]
    return rms_norm(x, final_norm_g)


_drawn_inputs = setup_inputs


def setup_inputs(seed=0):
    import zlib

    import numpy as np

    out = dict(_drawn_inputs(seed))
    spreads = {}
    factors = {'gmlp_ln_g': 3.389, 'gmlp_ln_b': 7.662}
    for name, (base, spread) in spreads.items():
        noise = np.random.default_rng([zlib.crc32(name.encode()), seed]).standard_normal(out[name].shape)
        drawn = base * np.exp(spread * noise) if base else spread * noise
        out[name] = __import__('jax').numpy.asarray(drawn.astype(out[name].dtype))
    for name, factor in factors.items():
        out[name] = (out[name] * factor).astype(out[name].dtype)
    return out
```

```python
from contextlib import ExitStack

import numpy as np

import concourse.bass as bass
from concourse import mybir

F32 = mybir.dt.float32
F32R = mybir.dt.float32r
F16 = mybir.dt.float16
ALU = mybir.AluOpType
ACT = mybir.ActivationFunctionType
AX_X = mybir.AxisListType.X

P = 128
D, S, DEPTH = 1024, 1024, 2
KT_D = D // P
HALF = 512
DH = 64
HA = D // (2 * DH)
HB = D // (4 * DH)
WA, WB = HA * DH, HB * DH
IN_W = 3 * WA + 2 * WB + WB
FF = -(-8 * D // (3 * 256)) * 256
FT = FF // P
NI = FT // 2
EPS = 1e-6
GW = 64
GROWS = S // GW
KH, KW = 8, 16
QR, QC = 8, 16
KR, KC = 12, 32
NKEY = KR * KC
NJ = GW // QC
BAND = [min(max(QC * j - KW // 2, 0), GW - KC) for j in range(NJ)]
BR, BC = 16, 48
BCOL = [BAND[j] - QC * j + QC for j in range(NJ)]
NEG = (-30528.0, 32768.0)

PROJ_SLOT = [p % 4 for p in range(18)]
OUT_SLOT = [4, 5, 0, 1, 2, 3, 4, 5]
PER_SLOT = [sum(s == t for t in PROJ_SLOT + OUT_SLOT) + NI for s in range(6)]


def nth_in_slot(seq, p, before=()):
    return sum(t == seq[p] for t in list(before) + list(seq[:p]))


GROUP_END = {3: 8, 7: 16, 11: 24, 15: 32, 17: 40, 21: 8, 25: 16}
ALL_SLOT = PROJ_SLOT + OUT_SLOT
USED = [sum(s == t and p not in GROUP_END for p, t in enumerate(ALL_SLOT)) for s in range(6)]
FFN_FIRST = [sum(s == t for t in PROJ_SLOT + OUT_SLOT) for s in range(6)]
OUT_ORDER = [4, 5, 6, 7, 0, 1, 2, 3]

SIL_CREDIT, GATED_CREDIT, SPLIT_CREDIT, ADD_CREDIT = 2, 2, 2, 20
GU_CREDIT, DN_CREDIT = 8, 16
FFT_STEPS = 13
ADDS = 16 * NI

KB = 1024
BASE = 16512
AT = dict(
    X=0, HH=32, HL=64,
    Q=96, K=112, AH=96, AL=104, SIL=112, TT=116,
    VN=128, UV=144, XC=160, BIAS=144, SQB=144,
    SQ=144, R=152, TN=156,
    Z=32, EO=40, MB=64, MC=72,
    AB=168, VB0=176, VB1=168, TW=184, MASK=184, L=190, PT=194.5, OT=197.5,
)
SLOT_AT = [168, 176, 184, 192, 128, 136]


def build(nc, x, win, wout, wg, wu, wd, bias, wsp, bsp, lng, lnb, gmix, ghead, gffn, gfin,
          tw, bd, onehot, mask, ident, out):
    ctx = ExitStack()
    with ctx:
        def at(name, kb, shape, dt=F32):
            return nc.alloc_sbuf_tensor_at(name, shape, dt, offset=BASE + int(kb * KB))

        X = at("x_res", AT["X"], [P, KT_D, S])
        HH = at("h_hi", AT["HH"], [P, KT_D, S], F32R)
        HL = at("h_lo", AT["HL"], [P, KT_D, S], F32R)
        QT = at("q_t", AT["Q"], [P, WA // P, S])
        KT = at("k_t", AT["K"], [P, WA // P, S])
        VN = at("v_tok", AT["VN"], [P, S // P, WA])
        UV = at("uv_tok", AT["UV"], [P, S // P, 2 * WB])
        XC = at("xc_tok", AT["XC"], [P, S // P, WB])
        BIAS = at("bias_rel", AT["BIAS"], [P, HA, BR, BC])
        SQB = at("mb_sq", AT["SQB"], [P, 32, DH])
        SQ = at("x_sq", AT["SQ"], [P, 4, HALF])
        R = at("rstd_bc", AT["R"], [P, 2, HALF])
        TN = at("x_normed", AT["TN"], [P, 2, HALF])
        Z = at("dft8", AT["Z"], [P, 8, WB])
        EO = at("dft8_even_odd", AT["EO"], [P, 8, WB])
        MB = at("mix_gate", AT["MB"], [P, 8, WB])
        MC = at("mix_fourier", AT["MC"], [P, 8, WB])
        AB = at("dft_t", AT["AB"], [P, 8, 256])
        VB = [at("v_band0", AT["VB0"], [P, 4, WA]), at("v_band1", AT["VB1"], [P, 4, WA])]
        TW = at("twiddle", AT["TW"], [P, 8, 2, 256])
        MASK = at("mask", AT["MASK"], [24, 2 * NJ, NKEY], F16)
        L = at("logits", AT["L"], [P, 3, NKEY])
        PT = at("probs_t", AT["PT"], [P, 2, NKEY])
        OT = at("att_tok", AT["OT"], [P, HA, DH])
        AH = at("act_hi", AT["AH"], [P, 2, S], F32R)
        AL = at("act_lo", AT["AL"], [P, 2, S], F32R)
        SIL = at("silu_g", AT["SIL"], [P, 2, HALF])
        TT = at("gated", AT["TT"], [P, 2, HALF])
        WH = [at(f"w_hi{s}", SLOT_AT[s], [P, 1024], F32R) for s in range(6)]
        WL = [at(f"w_lo{s}", SLOT_AT[s] + 4, [P, 1024], F32R) for s in range(6)]
        WR = [at(f"w_raw{s}", SLOT_AT[s] + 4, [P, 1024]) for s in range(6)]
        OUTS = at("out_t", AT["HH"], [P, KT_D, S])
        small = [200 * KB]

        def keep(name, shape, dt=F32):
            size = int(np.prod(shape[1:])) * (2 if dt == F16 else 4)
            t = nc.alloc_sbuf_tensor_at(name, shape, dt, offset=BASE + small[0])
            small[0] += -(-size // 32) * 32
            return t

        IDENT = keep("ident", [P, P])
        ONES = keep("ones", [P, P])
        BD = keep("channel_dft", [P, 2, P])
        ONEHOT = keep("onehot", [24, P], F16)
        WSP = keep("w_spatial_t", [P, HB, P])
        LNG = keep("ln_g", [P, WB])
        LNB = keep("ln_b", [P, WB])
        BSP = keep("b_spatial", [P, HB])
        GM = keep("g_mix", [P, KT_D])
        GH = keep("g_head", [P, KT_D])
        GF = keep("g_ffn", [P, KT_D])
        GO = keep("g_final", [P, KT_D])
        NHALF = keep("minus_half", [P, 32])
        ST = keep("bn_stats", [P, 8, 6])
        MV = keep("mean_var", [P, 8, 2])
        LR = keep("ln_rstd", [P, 8])
        SS = keep("head_ss", [P, 32])
        SR = keep("head_rstd", [P, 32])
        NM = keep("minus_max", [P, 4])
        SUM = keep("exp_sum", [P, 2, HA])
        RS = keep("exp_sum_inv", [P, HA])
        assert BASE + small[0] <= 229368

        B = [ctx.enter_context(nc.psum_tensor(f"bank{i}", [P, HALF], F32)) for i in range(8)]

        def sem(name):
            return ctx.enter_context(nc.semaphore(name))

        x_landed = [sem(f"x_landed{k}") for k in range(KT_D)]
        const_landed = sem("const_landed")
        layer_landed = sem("layer_landed")
        tw_landed, bias_landed, mask_landed = sem("tw_landed"), sem("bias_landed"), sem("mask_landed")
        vb_landed = [sem("vb_landed0"), sem("vb_landed1")]
        w_landed = [sem(f"w_landed{s}") for s in range(6)]
        w_hi = [sem(f"w_hi{s}") for s in range(6)]
        w_ready = [sem(f"w_ready{s}") for s in range(6)]
        w_used = [sem(f"w_used{s}") for s in range(6)]
        memsets = sem("memsets")
        dve_passed, sp_passed = sem("dve_passed"), sem("sp_passed")

        class Norm:

            def __init__(self, name):
                self.sq, self.ssq, self.v, self.r, self.t, self.hi, self.lo = (
                    sem(f"{name}_{x}") for x in ("sq", "ssq", "v", "r", "t", "hi", "lo"))

        n_mix, n_ffn, n_fin = Norm("nm"), Norm("nf"), Norm("no")
        acc_full, ev_act, ev_dve = sem("acc_full"), sem("ev_act"), sem("ev_dve")
        ln_stat, ln_var, ln_rstd, ln_step = sem("ln_stat"), sem("ln_var"), sem("ln_rstd"), sem("ln_step")
        sp_full, mb_made = sem("sp_full"), sem("mb_made")
        fft_step = sem("fft_step")
        dft_full, ab_made, cd_full, cd_done, mc_made = (
            sem("dft_full"), sem("ab_made"), sem("cd_full"), sem("cd_done"), sem("mc_made"))
        hs_sq, hs_red, hs_var, hs_rstd, hs_norm = (
            sem("hs_sq"), sem("hs_red"), sem("hs_var"), sem("hs_rstd"), sem("hs_norm"))
        bt_full, bt_hi, bt_lo = sem("bt_full"), sem("bt_hi"), sem("bt_lo")
        s_full, l_made, p_made, pt_full, pt_made, pv_done = (
            sem("s_full"), sem("l_made"), sem("p_made"), sem("pt_full"), sem("pt_made"), sem("pv_done"))
        o_inv, o_made, o_sq, o_red, o_var, o_rstd, o_norm = (
            sem("o_inv"), sem("o_made"), sem("o_sq"), sem("o_red"), sem("o_var"), sem("o_rstd"), sem("o_norm"))
        ot_full, ot_hi, ot_lo = sem("ot_full"), sem("ot_hi"), sem("ot_lo")
        out_full, out_added = sem("out_full"), sem("out_added")
        gu_full, sil_made, gated, a_hi, a_lo, dn_full, dn_added = (
            sem("gu_full"), sem("sil_made"), sem("gated"), sem("a_hi"), sem("a_lo"), sem("dn_full"),
            sem("dn_added"))
        out_ready, stored = sem("out_ready"), sem("stored")

        block = ctx.enter_context(nc.Block())

        def half(h):
            return slice(h * HALF, (h + 1) * HALF)

        def grid(ap):
            return ap.rearrange("p (r c) -> p r c", c=GW)

        MIX_TILES = [(k, h) for k in range(KT_D) for h in range(2)]
        FFN_TILES = [(k, h) for h in range(2) for k in range(KT_D)]

        def x_ready(e, l, k, h):
            e.wait_ge(x_landed[k], 16)
            e.wait_ge(dn_added, l * ADDS + (8 * h + k + 1 + ADD_CREDIT - 16))

        def x_mixed(e, l, k, h):
            e.wait_ge(out_added, l * 16 + (2 * k + h + 1))

        def qk_out(g, b):
            if g:
                return KT[:, b // 2, half(b % 2)]
            return QT[:, b // 2, :].rearrange("p (j h r c) -> p h r j c", j=NJ, h=2, c=QC)[:, b % 2]

        def qk_in(g, b):
            return B[b][:, :] if g else B[b][:, :].rearrange("p (r j c) -> p r j c", j=NJ, c=QC)

        def batch_out(t, b):
            k, q = 4 + b // 2, b % 2
            if b < 4:
                return t[:, k, half(q)]
            return t[:, k, :].rearrange("p (c a) -> p a c", a=8)[:, 4 * q:4 * q + 4, :]

        def batch_in(b):
            bank = B[6 + b % 2][:, :]
            return bank if b < 4 else bank.rearrange("p (a c) -> p a c", a=4)

        def tile_out(t, tile, k):
            j, rr = divmod(tile, 2)
            return grid(t[:, k, :])[:, QR * rr:QR * (rr + 1), QC * j:QC * (j + 1)]

        def tile_in(tile, k):
            return B[6 + tile % 2][:, k * P:(k + 1) * P].rearrange("p (r c) -> p r c", c=QC)

        @block.sync
        def _(sp):
            for k in range(KT_D):
                sp.dma_start(X[:, k, :], x[k]).then_inc(x_landed[k], 16)
            for dst, src in ((ONEHOT, onehot), (GO, gfin)):
                sp.dma_start(dst[:, :], src).then_inc(const_landed, 16)
            sp.dma_start(IDENT[:, :], ident).then_inc(const_landed, 16)
            sp.dma_start(BD[:, :, :], bd).then_inc(const_landed, 16)


            def passed():
                sp.sem_inc(sp_passed, 1)

            with sp.Fori(0, DEPTH) as l:
                sp.dma_start(GM[:, :], gmix[l]).then_inc(layer_landed, 16)
                sp.dma_start(GH[:, :], ghead[l]).then_inc(layer_landed, 16)
                sp.dma_start(GF[:, :], gffn[l]).then_inc(layer_landed, 16)
                sp.dma_start(LNG[:, :], lng[l]).then_inc(layer_landed, 16)
                sp.dma_start(LNB[:, :], lnb[l]).then_inc(layer_landed, 16)
                sp.dma_start(BSP[:, :], bsp[l]).then_inc(layer_landed, 16)
                sp.dma_start(WSP[:, :, :], wsp[l]).then_inc(layer_landed, 16)

                def wait_released(p):
                    passed()
                    s = ALL_SLOT[p]
                    if p not in GROUP_END:
                        nth = sum(ALL_SLOT[o] == s and o not in GROUP_END for o in range(p + 1))
                        sp.wait_ge(w_used[s], l * USED[s] + nth)
                    elif p < 18:
                        sp.wait_ge(acc_full, l * 40 + GROUP_END[p])
                    else:
                        sp.wait_ge(out_full, l * 16 + GROUP_END[p])

                def slot_free(p):
                    before = [o for o in range(p) if ALL_SLOT[o] == ALL_SLOT[p]]
                    if before:
                        wait_released(before[-1])
                    else:
                        sp.wait_ge(gu_full, l * (8 * NI) + GU_CREDIT)
                        passed()
                        sp.wait_ge(dn_full, l * (16 * NI) + DN_CREDIT)
                    passed()
                    return ALL_SLOT[p]

                for p in range(18):
                    s = slot_free(p)
                    if p < 16:
                        g, kk = p // 4, 2 * (p % 4)
                        src = win[l, kk:kk + 2, :, g * 512:(g + 1) * 512].rearrange("k p n -> p k n")
                        dst = WR[s][:, :].rearrange("p (k n) -> p k n", k=2)
                    else:
                        kk = 4 * (p - 16)
                        src = win[l, kk:kk + 4, :, 2048:2304].rearrange("k p n -> p k n")
                        dst = WR[s][:, :].rearrange("p (k n) -> p k n", k=4)
                    sp.dma_start(dst, src).then_inc(w_landed[s], 16)
                wait_released(14)
                wait_released(15)
                passed()
                sp.dma_start(TW[:, :, :, :], tw).then_inc(tw_landed, 16)
                passed()
                sp.wait_ge(ev_act, l * 28 + 12)
                passed()
                sp.wait_ge(ev_dve, l * 12 + 12)
                wait_released(17)

                def load_band(j):
                    for row in range(GROWS):
                        p0 = (row % 2) * GW + BAND[j]
                        q0 = (row % 4) * KC
                        sp.dma_start(VB[j % 2][q0:q0 + KC, row // 4, :],
                                     VN[p0:p0 + KC, row // 2, :]).then_inc(vb_landed[j % 2], 16)

                passed()
                load_band(0)
                sp.wait_ge(hs_red, l * 2 + 1)
                passed()
                sp.wait_ge(fft_step, l * FFT_STEPS + 2)
                passed()
                sp.dma_start(BIAS[:, :, :, :], bias[l]).then_inc(bias_landed, 16)
                sp.wait_ge(cd_full, l * 2 + 2)
                passed()
                sp.dma_start(MASK[:, :, :], mask).then_inc(mask_landed, 16)
                passed()
                load_band(1)
                sp.wait_ge(pv_done, l * 64 + 16)
                passed()
                load_band(2)
                sp.wait_ge(pv_done, l * 64 + 32)
                passed()
                load_band(3)
                for j in (0, 1):
                    sp.wait_ge(vb_landed[j], (l + 1) * 2 * GROWS * 16)
                    passed()
                for p in range(8):
                    s = slot_free(18 + p)
                    if p == 2:
                        sp.wait_ge(pv_done, l * 64 + 64)
                        passed()
                        sp.wait_ge(ot_full, l * 8 + 8)
                        passed()
                    g, kk = p // 4, OUT_ORDER[2 * (p % 4)]
                    sp.dma_start(WR[s][:, :].rearrange("p (k n) -> p k n", k=2),
                                 wout[l, kk:kk + 2, :, g * 512:(g + 1) * 512].rearrange("k p n -> p k n"))\
                      .then_inc(w_landed[s], 16)
                with sp.Fori(0, NI) as i:
                    for s in range(6):
                        wait_released((20, 21, 22, 23, 24, 25)[s])
                        passed()
                        if s < 4:
                            sp.wait_ge(gu_full, (l * NI + i) * 8 + (2 * s + 2 - 8 + GU_CREDIT))
                        else:
                            sp.wait_ge(dn_full, (l * NI + i) * 16 + DN_CREDIT)
                        passed()
                        src = (wg[l, 2 * i + s // 2] if s in (0, 2) else
                               wu[l, 2 * i + s // 2] if s in (1, 3) else wd[l, 2 * i + (s - 4)])
                        sp.dma_start(WR[s][:, :], src).then_inc(w_landed[s], 16)
            for h in range(2):
                for k in range(KT_D):
                    sp.wait_ge(out_ready, h * KT_D + k + 1)
                    sp.dma_start(out[k, :, half(h)], OUTS[:, k, half(h)]).then_inc(stored, 16)
            sp.wait_ge(stored, 16 * 16)

        @block.gpsimd
        def _(pool):
            nc.gpsimd.memset(ONES[:, :], 1.0).then_inc(memsets, 1)
            nc.gpsimd.memset(NHALF[:, :], -0.5).then_inc(memsets, 1)
            pool.wait_ge(memsets, 2)
            with pool.Fori(0, DEPTH) as l:
                def split_lo(s, nth):
                    pool.wait_ge(w_hi[s], nth)
                    nc.gpsimd.tensor_tensor(WL[s][:, :], WR[s][:, :], WH[s][:, :], ALU.subtract)\
                        .then_inc(w_ready[s], 1)

                for p in range(18):
                    split_lo(PROJ_SLOT[p], l * PER_SLOT[PROJ_SLOT[p]] + nth_in_slot(PROJ_SLOT, p) + 1)
                    if p == 17:
                        pool.wait_ge(ln_var, l + 1)
                        nc.gpsimd.tensor_tensor(LR[:, :], LR[:, :], NHALF[:, 0:8], ALU.pow).then_inc(ln_rstd, 1)
                for n in range(2):
                    pool.wait_ge(hs_var, l * 2 + n + 1)
                    nc.gpsimd.tensor_tensor(SR[:, :], SS[:, :], NHALF[:, :], ALU.pow).then_inc(hs_rstd, 1)
                for t in range(8):
                    pool.wait_ge(o_var, l * 8 + t + 1)
                    nc.gpsimd.tensor_tensor(SR[:, 0:HA], SS[:, 0:HA], NHALF[:, 0:HA], ALU.pow).then_inc(o_rstd, 1)
                for p in range(8):
                    s = OUT_SLOT[p]
                    split_lo(s, l * PER_SLOT[s] + nth_in_slot(OUT_SLOT, p, PROJ_SLOT) + 1)
                with pool.Fori(0, NI) as i:
                    for s in range(6):
                        split_lo(s, l * PER_SLOT[s] + i + (FFN_FIRST[s] + 1))

        @block.scalar
        def _(act):
            act.sem_inc(sil_made, SIL_CREDIT)
            act.sem_inc(a_hi, SPLIT_CREDIT)

            def norm_squares(n, l, ready):
                for i in range(16):
                    h, k = divmod(i, KT_D)
                    ready(act, k, h)
                    if i >= 4:
                        act.wait_ge(n.ssq, l * 16 + i - 3)
                    nc.scalar.activation(SQ[:, i % 4, :], X[:, k, half(h)], ACT.Square).then_inc(n.sq, 1)
                for h in range(2):
                    act.wait_ge(n.v, l * 4 + 2 * h + 2)
                    nc.scalar.activation(R[:, h, :], R[:, h, :], ACT.Sqrt).then_inc(n.r, 1)

            def norm_hi(n, l, tiles):
                for i, (k, h) in enumerate(tiles):
                    act.wait_ge(n.t, l * 16 + i + 1)
                    nc.scalar.activation(HH[:, k, half(h)], TN[:, i % 2, :], ACT.Copy).then_inc(n.hi, 1)

            def split_hi(s, nth):
                act.wait_ge(w_landed[s], nth * 16)
                nc.scalar.activation(WH[s][:, :], WR[s][:, :], ACT.Copy).then_inc(w_hi[s], 1)

            with act.Fori(0, DEPTH) as l:
                def proj_hi(p):
                    if p < 18:
                        s = PROJ_SLOT[p]
                        split_hi(s, l * PER_SLOT[s] + nth_in_slot(PROJ_SLOT, p) + 1)

                norm_squares(n_mix, l, lambda e, k, h: x_ready(e, l, k, h))
                proj_hi(0)
                for i, (k, h) in enumerate(MIX_TILES):
                    act.wait_ge(n_mix.t, l * 16 + i + 1)
                    nc.scalar.activation(HH[:, k, half(h)], TN[:, i % 2, :], ACT.Copy).then_inc(n_mix.hi, 1)
                    if i in (2, 6, 10):
                        proj_hi(1 + i // 4)

                for g in range(3):
                    for p in range(3):
                        proj_hi(4 * g + 4 + p)
                    for b in range(8):
                        if b % 2 == 0:
                            act.wait_ge(acc_full, l * 40 + g * 8 + b + 1)
                            if g < 2:
                                nc.scalar.activation(qk_out(g, b), qk_in(g, b), ACT.Copy,
                                                     scale=(DH ** -0.5, 1.0)[g]).then_inc(ev_act, 1)
                            else:
                                nc.scalar.activation(VN[:, b, :], B[b][:, :], ACT.Copy).then_inc(ev_act, 1)
                    proj_hi(4 * g + 7)
                proj_hi(16)
                proj_hi(17)
                for b in range(8):
                    act.wait_ge(acc_full, l * 40 + 24 + b + 1)
                    nc.scalar.activation(UV[:, b, :], B[b][:, :], ACT.Gelu_apprx_tanh).then_inc(ev_act, 1)
                for b in range(8):
                    act.wait_ge(acc_full, l * 40 + 32 + b + 1)
                    nc.scalar.activation(XC[:, b, :], B[b][:, 0:WB], ACT.Copy).then_inc(ev_act, 1)
                for b in range(4):
                    act.wait_ge(dft_full, l * 8 + b + 1)
                    nc.scalar.activation(AB[:, 2 * b:2 * b + 2, :], B[4 + b][:, :], ACT.Copy).then_inc(ab_made, 1)
                act.wait_ge(mb_made, l * 4 + 4)
                nc.scalar.activation(SQB[:, :, :], MB[:, :, :], ACT.Square).then_inc(hs_sq, 1)
                act.wait_ge(cd_full, l * 2 + 1)
                for b in range(4):
                    act.wait_ge(dft_full, l * 8 + 4 + b + 1)
                    nc.scalar.activation(AB[:, 2 * b:2 * b + 2, :], B[b][:, :], ACT.Copy).then_inc(ab_made, 1)
                act.wait_ge(cd_full, l * 2 + 2)
                for b in range(4):
                    nc.scalar.activation(MC[:, 2 * b:2 * b + 2, :], B[4 + b][:, :], ACT.Copy).then_inc(mc_made, 1)
                act.wait_ge(mc_made, l * 4 + 4)
                nc.scalar.activation(EO[:, :, :], MC[:, :, :], ACT.Square).then_inc(hs_sq, 1)

                for t in range(73):
                    if t < 64:
                        act.wait_ge(l_made, l * 64 + t + 1)
                        if t >= 16 and t % 8 == 0:
                            act.wait_ge(o_inv, l * 8 + t // 8 - 1)
                        nc.scalar.activation(L[:, t % 3, :], L[:, t % 3, :], ACT.Exp, scale=-1.0,
                                             bias=NM[:, t % 4:t % 4 + 1],
                                             accum_out=SUM[:, (t // 8) % 2, t % 8:t % 8 + 1]).then_inc(p_made, 1)
                    if t < 8:
                        k = 4 + t // 2
                        act.wait_ge(bt_full, l * 8 + t + 1)
                        nc.scalar.activation(batch_out(HH, t), batch_in(t), ACT.Copy,
                                             scale=GH[:, k:k + 1]).then_inc(bt_hi, 1)
                    tile, ph = divmod(t - 9, 8)
                    if t >= 11 and ph == 2:
                        act.wait_ge(o_made, l * 8 + tile + 1)
                        if tile < 2:
                            act.wait_ge(bt_lo, l * 8 + 7 + tile)
                        else:
                            act.wait_ge(ot_lo, l * 32 + 4 * (tile - 1))
                        nc.scalar.activation(B[6 + tile % 2][:, :].rearrange("p (h d) -> p h d", d=DH), OT[:, :, :],
                                             ACT.Square).then_inc(o_sq, 1)
                    if t >= 15 and ph == 6:
                        act.wait_ge(ot_full, l * 8 + tile + 1)
                        for k in range(4):
                            nc.scalar.activation(tile_out(HH, tile, k), tile_in(tile, k), ACT.Copy,
                                                 scale=GH[:, k:k + 1]).then_inc(ot_hi, 1)

                for p in range(8):
                    s = OUT_SLOT[p]
                    split_hi(s, l * PER_SLOT[s] + nth_in_slot(OUT_SLOT, p, PROJ_SLOT) + 1)
                norm_squares(n_ffn, l, lambda e, k, h: x_mixed(e, l, k, h))
                norm_hi(n_ffn, l, FFN_TILES)
                with act.Fori(0, NI) as i:
                    F = (l * NI + i) * 4
                    for s in range(4):
                        split_hi(s, l * PER_SLOT[s] + i + (FFN_FIRST[s] + 1))

                    def silu(f, h):
                        act.wait_ge(gu_full, (l * NI + i) * 8 + (4 * f + h + 1 + GU_CREDIT))
                        act.wait_ge(gated, F + (2 * f + h - 1 + GATED_CREDIT))
                        nc.scalar.activation(SIL[:, h, :], B[h][:, :], ACT.Silu).then_inc(sil_made, 1)

                    def gated_hi(f, h):
                        act.wait_ge(gated, F + (2 * f + h + 1 + GATED_CREDIT))
                        nc.scalar.activation(AH[:, f, half(h)], TT[:, h, :], ACT.Copy).then_inc(a_hi, 1)

                    silu(0, 0)
                    split_hi(4, l * PER_SLOT[4] + i + (FFN_FIRST[4] + 1))
                    silu(0, 1)
                    split_hi(5, l * PER_SLOT[5] + i + (FFN_FIRST[5] + 1))
                    gated_hi(0, 0)
                    gated_hi(0, 1)
                    silu(1, 0)
                    silu(1, 1)
                    gated_hi(1, 0)
                    gated_hi(1, 1)
            norm_squares(n_fin, 0, lambda e, k, h: e.wait_ge(
                dn_added, DEPTH * ADDS + ADD_CREDIT - 16 + 8 * h + k + 1))

        @block.vector
        def _(dve):
            dve.sem_inc(gated, GATED_CREDIT)
            dve.sem_inc(a_lo, SPLIT_CREDIT)
            dve.sem_inc(dn_added, ADD_CREDIT)

            def norm_var(n, l):
                for h in range(2):
                    dve.wait_ge(n.ssq, l * 16 + 8 * h + 8)
                    nc.vector.tensor_scalar(R[:, h, :], B[h][:, :], 1.0 / D, EPS, ALU.mult, ALU.add).then_inc(n.v, 1)
                    dve.wait_ge(n.v, l * 4 + 2 * h + 1)
                    nc.vector.reciprocal(R[:, h, :], R[:, h, :]).then_inc(n.v, 1)

            def norm_split(n, l, g, tiles):
                def lo(i):
                    k, h = tiles[i]
                    dve.wait_ge(n.hi, l * 16 + i + 1)
                    nc.vector.tensor_tensor(HL[:, k, half(h)], TN[:, i % 2, :], HH[:, k, half(h)],
                                            ALU.subtract).then_inc(n.lo, 1)

                for i, (k, h) in enumerate(tiles):
                    if i < 2:
                        dve.wait_ge(n.r, l * 2 + (tiles[i][1] if tiles[1][1] else 0) + 1)
                    if h == 1 and not tiles[1][1]:
                        dve.wait_ge(n.r, l * 2 + 2)
                    if i >= 2:
                        dve.wait_ge(n.lo, l * 16 + i - 1)
                    nc.vector.scalar_tensor_tensor(out=TN[:, i % 2, :], in0=X[:, k, half(h)], scalar=g[:, k:k + 1],
                                                   in1=R[:, h, :], op0=ALU.mult, op1=ALU.mult).then_inc(n.t, 1)
                    if i >= 1:
                        lo(i - 1)
                lo(15)

            with dve.Fori(0, DEPTH) as l:
                dve.wait_ge(layer_landed, (l + 1) * (7 * 16))
                norm_var(n_mix, l)
                norm_split(n_mix, l, GM, MIX_TILES)
                for g in range(3):
                    for b in range(1, 8, 2):
                        dve.wait_ge(acc_full, l * 40 + g * 8 + b + 1)
                        if g < 2:
                            nc.vector.tensor_scalar(qk_out(g, b), qk_in(g, b),
                                                    (DH ** -0.5, 1.0)[g], None, ALU.mult).then_inc(ev_dve, 1)
                        else:
                            nc.vector.tensor_copy(VN[:, b, :], B[b][:, :]).then_inc(ev_dve, 1)
                for b in range(8):
                    dve.wait_ge(ev_act, l * 28 + 12 + b + 1)
                    nc.vector.bn_stats(ST[:, b, :], UV[:, b, WB:2 * WB]).then_inc(ln_stat, 1)
                    dve.wait_ge(ln_stat, l * 16 + 2 * b + 1)
                    dve.sem_inc(dve_passed, 1)
                    nc.vector.bn_aggr(MV[:, b, :], ST[:, b, :]).then_inc(ln_stat, 1)
                dve.wait_ge(ln_stat, l * 16 + 16)
                nc.vector.tensor_scalar(LR[:, :], MV[:, :, 1], EPS, None, ALU.add).then_inc(ln_var, 1)
                dve.wait_ge(ln_rstd, l + 1)
                for b in range(8):
                    nc.vector.tensor_scalar(UV[:, b, WB:2 * WB], UV[:, b, WB:2 * WB], MV[:, b, 0:1], LR[:, b:b + 1],
                                            ALU.subtract, ALU.mult).then_inc(ln_step, 1)
                dve.wait_ge(ln_step, l * 10 + 8)
                nc.vector.tensor_tensor(UV[:, :, WB:2 * WB], UV[:, :, WB:2 * WB],
                                        LNG[:, :].rearrange("p (a n) -> p a n", a=1).to_broadcast([P, 8, WB]),
                                        ALU.mult).then_inc(ln_step, 1)
                dve.wait_ge(ln_step, l * 10 + 9)
                nc.vector.tensor_tensor(UV[:, :, WB:2 * WB], UV[:, :, WB:2 * WB],
                                        LNB[:, :].rearrange("p (a n) -> p a n", a=1).to_broadcast([P, 8, WB]),
                                        ALU.add).then_inc(ln_step, 1)

                step = [0]

                def fft(ins, wait=False):
                    ins.then_inc(fft_step, 1)
                    step[0] += 1
                    if wait:
                        dve.wait_ge(fft_step, l * FFT_STEPS + step[0])

                dve.wait_ge(ev_act, l * 28 + 28)
                fft(nc.vector.tensor_tensor(EO[:, 0:4, :], XC[:, 0:4, :], XC[:, 4:8, :], ALU.add))
                fft(nc.vector.tensor_tensor(EO[:, 4:8, :], XC[:, 0:4, :], XC[:, 4:8, :], ALU.subtract), True)
                T = AB
                fft(nc.vector.tensor_tensor(T[:, 0:2, :], EO[:, 0:2, :], EO[:, 2:4, :], ALU.add))
                fft(nc.vector.tensor_tensor(T[:, 2, :], EO[:, 5, :], EO[:, 7, :], ALU.subtract))
                fft(nc.vector.tensor_tensor(T[:, 3, :], EO[:, 5, :], EO[:, 7, :], ALU.add))
                fft(nc.vector.tensor_tensor(Z[:, 2, :], EO[:, 0, :], EO[:, 2, :], ALU.subtract))
                fft(nc.vector.tensor_tensor(Z[:, 6, :], EO[:, 3, :], EO[:, 1, :], ALU.subtract), True)
                fft(nc.vector.tensor_tensor(Z[:, 0, :], T[:, 0, :], T[:, 1, :], ALU.add))
                fft(nc.vector.tensor_tensor(Z[:, 4, :], T[:, 0, :], T[:, 1, :], ALU.subtract))
                c = 0.5 ** 0.5
                for z, t, s, o, op in ((1, 2, c, 4, ALU.add), (3, 2, -c, 4, ALU.add),
                                       (5, 3, -c, 6, ALU.subtract), (7, 3, -c, 6, ALU.add)):
                    fft(nc.vector.scalar_tensor_tensor(out=Z[:, z, :], in0=T[:, t, :], scalar=s, in1=EO[:, o, :],
                                                       op0=ALU.mult, op1=op))
                assert step[0] == FFT_STEPS

                for h in range(HB):
                    dve.wait_ge(sp_full, l * HB + h + 1)
                    nc.vector.scalar_tensor_tensor(
                        out=MB[:, :, h * DH:(h + 1) * DH], in0=B[h][:, :].rearrange("p (n d) -> p n d", d=DH),
                        scalar=BSP[:, h:h + 1], in1=UV[:, :, h * DH:(h + 1) * DH],
                        op0=ALU.add, op1=ALU.mult).then_inc(mb_made, 1)

                def head_norm(n, m, sq):
                    dve.wait_ge(hs_sq, l * 2 + n + 1)
                    if n:
                        dve.wait_ge(hs_rstd, l * 2 + n)
                    nc.vector.tensor_reduce(SS[:, :], sq, AX_X, ALU.add).then_inc(hs_red, 1)
                    dve.wait_ge(hs_red, l * 2 + n + 1)
                    nc.vector.tensor_scalar(SS[:, :], SS[:, :], 1.0 / DH, EPS, ALU.mult, ALU.add).then_inc(hs_var, 1)

                def head_scale(n, m):
                    dve.wait_ge(hs_rstd, l * 2 + n + 1)
                    v = m[:, :, :].rearrange("p n (h d) -> p (n h) d", d=DH)
                    nc.vector.tensor_tensor(v, v, SR[:, :].rearrange("p (g a) -> p g a", a=1)
                                            .to_broadcast([P, 32, DH]), ALU.mult).then_inc(hs_norm, 1)

                head_norm(0, MB, SQB[:, :, :])
                head_scale(0, MB)
                dve.wait_ge(hs_norm, l * 2 + 1)
                head_norm(1, MC, EO[:, :, :].rearrange("p n (h d) -> p (n h) d", d=DH))

                for t in range(73):
                    if t == 0:
                        dve.wait_ge(bias_landed, (l + 1) * 16)
                    if t < 64:
                        j, rr, h = t // 16, (t // 8) % 2, t % 8
                        dve.wait_ge(s_full, l * 64 + t + 1)
                        if t >= 3:
                            dve.wait_ge(pt_full, l * 64 + t - 2)
                        dve.sem_inc(dve_passed, 1)
                        r0, c0 = 4 * (1 - rr), BCOL[j]
                        nc.vector.tensor_tensor_reduce(
                            L[:, t % 3, :].rearrange("p (r c) -> p r c", c=KC),
                            B[t % 2][:, 0:NKEY].rearrange("p (r c) -> p r c", c=KC),
                            BIAS[:, h, r0:r0 + KR, c0:c0 + KC], -1.0, 3e38, ALU.add, ALU.min,
                            NM[:, t % 4:t % 4 + 1]).then_inc(l_made, 1)
                    if 2 <= t <= 65:
                        u = t - 2
                        dve.wait_ge(pt_full, l * 64 + u + 1)
                        if u >= 2:
                            dve.wait_ge(pv_done, l * 64 + u - 1)
                        nc.vector.tensor_copy(PT[:, u % 2, :], B[2 + u % 2][:, 0:NKEY]).then_inc(pt_made, 1)
                    if t == 2:
                        head_scale(1, MC)
                    if 1 <= t <= 8:
                        b = t - 1
                        k = 4 + b // 2
                        dve.wait_ge(bt_hi, l * 8 + b + 1)
                        nc.vector.scalar_tensor_tensor(out=batch_out(HL, b), in0=batch_in(b), scalar=GH[:, k:k + 1],
                                                       in1=batch_out(HH, b), op0=ALU.mult,
                                                       op1=ALU.subtract).then_inc(bt_lo, 1)
                    tile, ph = divmod(t - 9, 8)
                    if t >= 11 and ph == 2:
                        dve.wait_ge(p_made, l * 64 + 8 * tile + 8)
                        nc.vector.reciprocal(RS[:, :], SUM[:, tile % 2, :]).then_inc(o_inv, 1)
                        dve.wait_ge(o_inv, l * 8 + tile + 1)
                        dve.wait_ge(pv_done, l * 64 + 8 * tile + 8)
                        if tile:
                            dve.wait_ge(ot_full, l * 8 + tile)
                        nc.vector.tensor_tensor(OT[:, :, :], B[4 + tile % 2][:, :].rearrange("p (h d) -> p h d", d=DH),
                                                RS[:, :].rearrange("p (h a) -> p h a", a=1).to_broadcast([P, HA, DH]),
                                                ALU.mult).then_inc(o_made, 1)
                    if t >= 12 and ph == 3:
                        if tile:
                            dve.wait_ge(o_norm, l * 8 + tile)
                        else:
                            dve.wait_ge(hs_norm, l * 2 + 2)
                        dve.wait_ge(o_sq, l * 8 + tile + 1)
                        nc.vector.tensor_reduce(SS[:, 0:HA], B[6 + tile % 2][:, :].rearrange("p (h d) -> p h d", d=DH),
                                                AX_X, ALU.add).then_inc(o_red, 1)
                        dve.wait_ge(o_red, l * 8 + tile + 1)
                        nc.vector.tensor_scalar(SS[:, 0:HA], SS[:, 0:HA], 1.0 / DH, EPS, ALU.mult,
                                                ALU.add).then_inc(o_var, 1)
                    if t >= 14 and ph == 5:
                        dve.wait_ge(o_rstd, l * 8 + tile + 1)
                        nc.vector.tensor_tensor(OT[:, :, :], OT[:, :, :],
                                                SR[:, 0:HA].rearrange("p (h a) -> p h a", a=1)
                                                .to_broadcast([P, HA, DH]), ALU.mult).then_inc(o_norm, 1)
                    if t >= 16 and ph == 7:
                        for k in range(4):
                            dve.wait_ge(ot_hi, l * 32 + 4 * tile + 4)
                            nc.vector.scalar_tensor_tensor(out=tile_out(HL, tile, k), in0=tile_in(tile, k),
                                                           scalar=GH[:, k:k + 1], in1=tile_out(HH, tile, k),
                                                           op0=ALU.mult, op1=ALU.subtract).then_inc(ot_lo, 1)
                for g in range(2):
                    for b in range(8):
                        k, h = 4 * g + b // 2, b % 2
                        dve.wait_ge(out_full, l * 16 + g * 8 + b + 1)
                        nc.vector.tensor_tensor(X[:, k, half(h)], B[b][:, :], X[:, k, half(h)],
                                                ALU.add).then_inc(out_added, 1)
                norm_var(n_ffn, l)
                norm_split(n_ffn, l, GF, FFN_TILES)
                with dve.Fori(0, NI) as i:
                    F = (l * NI + i) * 4
                    for f in range(2):
                        for h in range(2):
                            dve.wait_ge(sil_made, F + (2 * f + h + 1 + SIL_CREDIT))
                            dve.wait_ge(gu_full, (l * NI + i) * 8 + (4 * f + 2 + h + 1 + GU_CREDIT))
                            dve.wait_ge(a_hi, F + (2 * f + h - 1 + SPLIT_CREDIT))
                            dve.wait_ge(a_lo, F + (2 * f + h - 1 + SPLIT_CREDIT))
                            nc.vector.tensor_tensor(TT[:, h, :], B[2 + h][:, :], SIL[:, h, :], ALU.mult)\
                                .then_inc(gated, 1)
                            dve.wait_ge(a_hi, F + (2 * f + h + 1 + SPLIT_CREDIT))
                            nc.vector.tensor_tensor(AL[:, f, half(h)], TT[:, h, :], AH[:, f, half(h)], ALU.subtract)\
                                .then_inc(a_lo, 1)
                    for n in range(16):
                        h, k = divmod(n, 8)
                        dve.wait_ge(dn_full, (l * NI + i) * 16 + (n + 1 + DN_CREDIT))
                        nc.vector.tensor_tensor(X[:, k, half(h)], B[4 + n % 4][:, :], X[:, k, half(h)], ALU.add)\
                            .then_inc(dn_added, 1)
            norm_var(n_fin, 0)
            for h in range(2):
                dve.wait_ge(n_fin.r, h + 1)
                for k in range(KT_D):
                    nc.vector.scalar_tensor_tensor(out=OUTS[:, k, half(h)], in0=X[:, k, half(h)],
                                                   scalar=GO[:, k:k + 1], in1=R[:, h, :],
                                                   op0=ALU.mult, op1=ALU.mult).then_inc(out_ready, 1)

        @block.tensor
        def _(pe):
            pe.sem_inc(gu_full, GU_CREDIT)
            pe.sem_inc(dn_full, DN_CREDIT)
            pe.wait_ge(memsets, 2)
            pe.wait_ge(const_landed, 4 * 16)

            def norm_sum(n, l):
                for i in range(16):
                    h, k = divmod(i, KT_D)
                    if n is n_ffn and k == 0:
                        pe.wait_ge(out_added, l * 16 + 8 + h + 1)
                    pe.wait_ge(n.sq, l * 16 + i + 1)
                    nc.tensor.matmul(B[h][:, :], ONES[:, :], SQ[:, i % 4, :], start=(k == 0), stop=(k == KT_D - 1))\
                        .then_inc(n.ssq, 1)

            def split3(bank, lh, ll, rh, rl, start, stop):
                nc.tensor.matmul(bank, lh, rh, start=start, stop=False)
                nc.tensor.matmul(bank, lh, rl, start=False, stop=False)
                return nc.tensor.matmul(bank, ll, rh, start=False, stop=stop)

            with pe.Fori(0, DEPTH) as l:
                norm_sum(n_mix, l)

                def wait_piece(seq, p, before=()):
                    s = seq[p]
                    pe.wait_ge(w_ready[s], l * PER_SLOT[s] + nth_in_slot(seq, p, before) + 1)
                    return s

                def bank_free(g, b):
                    if 1 <= g <= 3:
                        if b % 2 == 0:
                            pe.wait_ge(ev_act, l * 28 + (g - 1) * 4 + b // 2 + 1)
                        else:
                            pe.wait_ge(ev_dve, l * 12 + (g - 1) * 4 + b // 2 + 1)
                    elif g == 4:
                        pe.wait_ge(ev_act, l * 28 + 12 + b + 1)

                for g in range(5):
                    per = 2 if g < 4 else 4
                    n = 512 if g < 4 else WB
                    for k in range(KT_D):
                        p = 4 * g + k // per
                        s = wait_piece(PROJ_SLOT, p) if k % per == 0 else PROJ_SLOT[p]
                        wh = WH[s][:, (k % per) * n:(k % per + 1) * n]
                        wl = WL[s][:, (k % per) * n:(k % per + 1) * n]
                        if g == 0:
                            pe.wait_ge(n_mix.lo, l * 16 + 2 * k + 2)
                        for b in range(8):
                            if k == 0:
                                bank_free(g, b)
                            if g < 2:
                                m, h = slice(b // 2 * P, (b // 2 + 1) * P), half(b % 2)
                                mm = split3(B[b][:, :], wh[:, m], wl[:, m], HH[:, k, h], HL[:, k, h],
                                            k == 0, k == KT_D - 1)
                            else:
                                m = slice(b * P, (b + 1) * P)
                                mm = split3(B[b][:, 0:n], HH[:, k, m], HL[:, k, m], wh, wl,
                                            k == 0, k == KT_D - 1)
                            if k == KT_D - 1:
                                mm.then_inc(acc_full, 1)
                        if k % per == per - 1 and p not in GROUP_END:
                            mm.then_inc(w_used[s], 1)

                pe.wait_ge(layer_landed, (l + 1) * (7 * 16))
                pe.wait_ge(ln_step, l * 10 + 10)
                for h in range(HB):
                    pe.wait_ge(ev_act, l * 28 + 20 + h + 1)
                    nc.tensor.matmul(B[h][:, :].rearrange("p (n d) -> p n d", d=DH), WSP[:, h, :],
                                     UV[:, :, WB + h * DH:WB + (h + 1) * DH], start=True, stop=True)\
                        .then_inc(sp_full, 1)

                def position_dft(f, banks):
                    m = slice(f * P, (f + 1) * P)
                    for a in range(8):
                        bank = B[banks + a // 2][:, (a % 2) * 256:(a % 2 + 1) * 256]
                        zr, zi = min(a, 8 - a), 4 + min(a, 8 - a)
                        both = a not in (0, 4)
                        mm = nc.tensor.matmul(bank, Z[:, zr, m], TW[:, a, 0, :], start=True, stop=not both)
                        if both:
                            mm = nc.tensor.matmul(bank, Z[:, zi, m], TW[:, a, 1, :], start=False, stop=True)
                        if a % 2:
                            mm.then_inc(dft_full, 1)

                def channel_dft(f):
                    for a in range(8):
                        pe.wait_ge(ab_made, l * 8 + 4 * f + a // 2 + 1)
                        bank = B[4 + a // 2][:, (a % 2) * 256 + f * P:(a % 2) * 256 + (f + 1) * P]
                        nc.tensor.matmul(bank, AB[:, a, 0:P], BD[:, 0, :], start=True, stop=False)
                        mm = nc.tensor.matmul(bank, AB[:, a, P:2 * P], BD[:, 1, :], start=False, stop=True)
                    mm.then_inc(cd_full, 1)

                pe.wait_ge(fft_step, (l + 1) * FFT_STEPS)
                pe.wait_ge(tw_landed, (l + 1) * 16)
                for b in range(4, 8):
                    pe.wait_ge(ev_act, l * 28 + 20 + b + 1)
                position_dft(0, 4)
                pe.wait_ge(mb_made, l * 4 + 4)
                position_dft(1, 0)
                channel_dft(0)
                channel_dft(1)

                def scores(t):
                    j, rr, h = t // 16, (t // 8) % 2, t % 8
                    bank = B[t % 2][:, 0:NKEY]
                    if t >= 2:
                        pe.wait_ge(l_made, l * 64 + t - 1)
                    else:
                        pe.wait_ge(ab_made, l * 8 + 8)
                    hp = slice(DH * (h % 2), DH * (h % 2) + DH)
                    nc.tensor.matmul(bank, ONEHOT[:, :], MASK[:, rr * NJ + j, :], start=True, stop=False)
                    q = QT[hp, h // 2, t // 8 * P:(t // 8 + 1) * P]
                    k = grid(KT[hp, h // 2, :])[:, 4 * rr:4 * rr + KR, BAND[j]:BAND[j] + KC]
                    nc.tensor.matmul(bank.rearrange("p (r c) -> p r c", c=KC), q, k,
                                     start=False, stop=True).then_inc(s_full, 1)

                def turn_probs(t):
                    pe.wait_ge(p_made, l * 64 + t + 1)
                    if t >= 2:
                        pe.wait_ge(pt_made, l * 64 + t - 1)
                    for n in range(3):
                        mm = nc.tensor.transpose(B[2 + t % 2][:, n * P:(n + 1) * P], L[:, t % 3, n * P:(n + 1) * P],
                                                 IDENT[:, :])
                    mm.then_inc(pt_full, 1)

                def values(t):
                    j, rr, h = t // 16, (t // 8) % 2, t % 8
                    pe.wait_ge(pt_made, l * 64 + t + 1)
                    if t % 16 == 0:
                        pe.wait_ge(vb_landed[j % 2], l * (2 * GROWS * 16) + (j // 2 + 1) * GROWS * 16)
                    if h == 0 and t >= 16:
                        pe.wait_ge(o_made, l * 8 + t // 8 - 1)
                    if t < 16 and h == 0:
                        pe.wait_ge(mc_made, l * 4 + 4)
                    cols = slice(h * DH, min(h + 2, HA) * DH)
                    for n in range(3):
                        mm = nc.tensor.matmul(B[4 + (t // 8) % 2][:, cols],
                                              PT[:, t % 2, n * P:(n + 1) * P],
                                              VB[j % 2][:, rr + n, cols],
                                              start=(n == 0), stop=(n == 2))
                    mm.then_inc(pv_done, 1)

                def turn_batch(b):
                    pe.wait_ge(hs_norm, l * 2 + b // 4 + 1)
                    if b < 2:
                        pe.wait_ge(mc_made, l * 4 + 4)
                    else:
                        pe.wait_ge(bt_lo, l * 8 + b - 1)
                    src = (MB, MC)[b // 4]
                    f, q = divmod(b % 4, 2)
                    for n in range(4):
                        mm = nc.tensor.transpose(B[6 + b % 2][:, n * P:(n + 1) * P],
                                                 src[:, 4 * q + n, f * P:(f + 1) * P], IDENT[:, :])
                    mm.then_inc(bt_full, 1)

                pe.wait_ge(mask_landed, (l + 1) * 16)
                for t in range(73):
                    if t < 64:
                        scores(t)
                    if 2 <= t <= 65:
                        turn_probs(t - 2)
                    if t < 8:
                        turn_batch(t)
                    if 3 <= t <= 66:
                        values(t - 3)
                    tile, ph = divmod(t - 9, 8)
                    if t >= 15 and ph == 6:
                        pe.wait_ge(o_norm, l * 8 + tile + 1)
                        for k in range(4):
                            mm = nc.tensor.transpose(B[6 + tile % 2][:, k * P:(k + 1) * P],
                                                     OT[:, 2 * k:2 * k + 2, :].rearrange("p h d -> p (h d)"),
                                                     IDENT[:, :])
                        mm.then_inc(ot_full, 1)

                pe.wait_ge(bt_lo, l * 8 + 8)
                for g in range(2):
                    for n, k in enumerate(OUT_ORDER):
                        p = 4 * g + n // 2
                        s = wait_piece(OUT_SLOT, p, PROJ_SLOT) if n % 2 == 0 else OUT_SLOT[p]
                        if g == 0 and n == 0:
                            pe.wait_ge(ot_lo, l * 32 + 32)
                        for b in range(8):
                            if n == 0 and g == 1:
                                pe.wait_ge(out_added, l * 16 + b + 1)
                            m, h = slice((n % 2) * 512 + b // 2 * P, (n % 2) * 512 + (b // 2 + 1) * P), half(b % 2)
                            mm = split3(B[b][:, :], WH[s][:, m], WL[s][:, m], HH[:, k, h], HL[:, k, h],
                                        n == 0, n == KT_D - 1)
                            if n == KT_D - 1:
                                mm.then_inc(out_full, 1)
                        if n % 2 and 18 + p not in GROUP_END:
                            mm.then_inc(w_used[s], 1)

                norm_sum(n_ffn, l)
                with pe.Fori(0, NI) as i:
                    F = (l * NI + i) * 4
                    for f in range(2):
                        for g in range(2):
                            s = 2 * f + g
                            pe.wait_ge(w_ready[s], l * PER_SLOT[s] + i + (FFN_FIRST[s] + 1))
                            for h in range(2):
                                pe.wait_ge(gated if g else sil_made, F + (2 * f + h - 1 + GATED_CREDIT))
                                for k in range(KT_D):
                                    if f == 0 and g == 0:
                                        pe.wait_ge(n_ffn.lo, l * 16 + (h * KT_D + k + 1))
                                    m = slice(k * P, (k + 1) * P)
                                    mm = split3(B[2 * g + h][:, :], WH[s][:, m], WL[s][:, m],
                                                HH[:, k, half(h)], HL[:, k, half(h)], k == 0, k == KT_D - 1)
                                mm.then_inc(gu_full, 1)
                    for s in (4, 5):
                        pe.wait_ge(w_ready[s], l * PER_SLOT[s] + i + (FFN_FIRST[s] + 1))
                    for n in range(16):
                        h, k = divmod(n, 8)
                        if n in (0, 8):
                            pe.wait_ge(a_lo, F + (2 + h + 1 + SPLIT_CREDIT))
                        pe.wait_ge(dn_added, (l * NI + i) * 16 + (n - 3 + ADD_CREDIT))
                        m = slice(k * P, (k + 1) * P)
                        for f in range(2):
                            mm = split3(B[4 + n % 4][:, :], WH[4 + f][:, m], WL[4 + f][:, m],
                                        AH[:, f, half(h)], AL[:, f, half(h)], f == 0, f == 1)
                        mm.then_inc(dn_full, 1)
            norm_sum(n_fin, 0)


def constants():
    b = np.arange(P)[:, None, None]
    a = np.arange(8)[None, :, None]
    c = np.arange(P)[None, None, :]
    th = 2 * np.pi * (b * (a + 8 * c) % S) / S
    sign = np.where(np.arange(8) > 4, -1.0, 1.0)[None, :, None]
    tw = np.stack([np.concatenate([np.cos(th), -np.sin(th)], 2),
                   np.concatenate([np.sin(th), np.cos(th)], 2) * sign], 2)
    f = np.arange(P)
    same = f[:, None] // DH == f[None, :] // DH
    ph = 2 * np.pi * ((f[:, None] % DH) * (f[None, :] % DH) % DH) / DH
    scale = (S * DH) ** -0.5
    bd = np.stack([np.cos(ph) * same * scale, np.sin(ph) * same * scale], 1)
    onehot = np.zeros((24, P), np.float32)
    qr, qc = np.divmod(np.arange(P), QC)
    onehot[qr, np.arange(P)] = NEG[1]
    onehot[8 + qc, np.arange(P)] = NEG[1]
    mask = np.zeros((24, 2, NJ, KR, KC), np.float32)
    for rr in range(2):
        key = 4 * rr + np.arange(KR)
        for q in range(QR):
            first = min(max(QR * rr + q - KH // 2, 0), GROWS - KH)
            mask[q, rr, :, (key < first) | (key >= first + KH), :] = NEG[0]
    for j in range(NJ):
        key = BAND[j] + np.arange(KC)
        for q in range(QC):
            first = min(max(QC * j + q - KW // 2, 0), GW - KW)
            mask[8 + q, :, j, :, (key < first) | (key >= first + KW)] = NEG[0]
    return dict(tw=tw.astype(np.float32), bd=bd.astype(np.float32), ident=np.eye(P, dtype=np.float32),
                onehot=onehot.astype(np.float16),
                mask=mask.reshape(24, 2 * NJ, NKEY).astype(np.float16))


def features(g):
    return np.ascontiguousarray(np.swapaxes(g.reshape(g.shape[:-1] + (KT_D, P)), -1, -2))


def lay_out(x, norm_mix_g, w_in, rpb, gmlp_ln_g, gmlp_ln_b, w_spatial, b_spatial, head_norm_g, w_out,
            norm_ffn_g, w_gate, w_up, w_down, final_norm_g):
    ff = (DEPTH, KT_D, P, FT, P)
    pad = np.pad(rpb, ((0, 0), (0, 0), (4, 4), (16, 16)))
    qr, qc = np.divmod(np.arange(P), QC)
    rows = np.arange(BR)[None, :] - qr[:, None] + 7
    cols = np.arange(BC)[None, :] - qc[:, None] + 15
    bias = pad[:, :, rows[:, :, None], cols[:, None, :]]
    return dict(
        x=np.ascontiguousarray(x[0].T).reshape(KT_D, P, S),
        win=w_in.reshape(DEPTH, KT_D, P, IN_W), wout=w_out.reshape(DEPTH, KT_D, P, D),
        wg=np.ascontiguousarray(w_gate.reshape(ff).transpose(0, 3, 2, 1, 4)).reshape(DEPTH, FT, P, D),
        wu=np.ascontiguousarray(w_up.reshape(ff).transpose(0, 3, 2, 1, 4)).reshape(DEPTH, FT, P, D),
        wd=w_down.reshape(DEPTH, FT, P, D),
        bias=np.ascontiguousarray(bias.transpose(0, 2, 1, 3, 4)),
        wsp=np.ascontiguousarray(w_spatial.transpose(0, 3, 1, 2)),
        bsp=np.ascontiguousarray(b_spatial.transpose(0, 2, 1)),
        lng=np.ascontiguousarray(np.broadcast_to(gmlp_ln_g[:, None], (DEPTH, P, WB))),
        lnb=np.ascontiguousarray(np.broadcast_to(gmlp_ln_b[:, None], (DEPTH, P, WB))),
        gmix=features(norm_mix_g), ghead=features(head_norm_g), gffn=features(norm_ffn_g),
        gfin=features(final_norm_g), **constants())


def kernel(**inputs):
    import concourse.bacc as bacc
    from concourse.bass_utils import run_bass_kernel_spmd

    nc = bacc.Bacc("TRN2", target_bir_lowering=False, num_devices=1)
    arrays = lay_out(**{k: np.asarray(v) for k, v in inputs.items()})
    args = {n: nc.dram_tensor(f"in_{n}", a.shape, mybir.dt.from_np(a.dtype), kind="ExternalInput").ap()
            for n, a in arrays.items()}
    args["out"] = nc.dram_tensor("out_t_dram", (KT_D, P, S), F32, kind="ExternalOutput").ap()
    build(nc, **args)
    got = run_bass_kernel_spmd(nc, [{f"in_{n}": a for n, a in arrays.items()}], core_ids=[0])
    return np.ascontiguousarray(got.results[0]["out_t_dram"].reshape(D, S).T)[None]
```

```python
from contextlib import ExitStack

import numpy as np

import concourse.bass as bass
from concourse import mybir

F32 = mybir.dt.float32
F32R = mybir.dt.float32r
F16 = mybir.dt.float16
ALU = mybir.AluOpType
ACT = mybir.ActivationFunctionType
AX_X = mybir.AxisListType.X

P = 128
D, S, DEPTH = 1024, 1024, 2
KT_D = D // P
HALF = 512
DH = 64
HA = D // (2 * DH)
HB = D // (4 * DH)
WA, WB = HA * DH, HB * DH
IN_W = 3 * WA + 2 * WB + WB
FF = -(-8 * D // (3 * 256)) * 256
FT = FF // P
NI = FT // 2
EPS = 1e-6
GW = 64
GROWS = S // GW
KH, KW = 8, 16
QR, QC = 8, 16
KR, KC = 12, 32
NKEY = KR * KC
NJ = GW // QC
COMBO = [0, 1, 1, 2]
BAND = [min(max(QC * j - KW // 2, 0), GW - KC) for j in range(NJ)]
BR, BC = 16, 48
BCOL = [BAND[j] - QC * j + QC for j in range(NJ)]
NEG = (-30528.0, 32768.0)

ALL_SLOT = [0, 1, 2, 0, 1, 2, 0, 1, 2, 0, 1, 2, 0, 1, 6, 0, 6, 0] + [7, 4, 5, 1, 2, 3, 0, 7]
OUT_P = 18
GROUPS = ("xc", "z", "q", "k", "v")
FIRST_P = (0, 2, 6, 10, 14, OUT_P)
COLUMN = dict(q=0, k=512, v=1024, z=1536, xc=2048)
SLOTS = 8
GROUP_END = {1: 8, 5: 16, 9: 24, 13: 32, 17: 40, 21: 8, 25: 16}
USED = [sum(s == t and p not in GROUP_END for p, t in enumerate(ALL_SLOT)) for s in range(SLOTS)]
FFN_FIRST = [sum(s == t for t in ALL_SLOT) for s in range(SLOTS)]
PER_SLOT = [FFN_FIRST[s] + (NI if s < 6 else 0) for s in range(SLOTS)]
LAST_P = [max(p for p, t in enumerate(ALL_SLOT) if t == s) for s in range(6)]


def nth_in_slot(p):
    return sum(t == ALL_SLOT[p] for t in ALL_SLOT[:p])


BANKS = [4, 5, 6, 7, 0, 1, 2, 3]
OUT_ORDER = [4, 5, 6, 7, 0, 1, 2, 3]

GATE_CREDIT, UP_CREDIT, GATED_CREDIT, SPLIT_CREDIT, ADD_CREDIT = 2, 2, 2, 2, 20
GU_CREDIT, DN_CREDIT = 8, 16
FFT_STEPS = 13
ADDS = 16 * NI

KB = 1024
BASE = 16512
AT = dict(
    X=0, HH=32, HL=64,
    Q=96, K=112, AH=96, AL=104, SIL=112, TT=116, SQ=120,
    TW=96, EO=112, Z=120, T=128, AB=128, SQB=128,
    VN=128, UV=144, XC=160, VB0=152, VB1=160,
    XG=152, ACC=160, RF=164, RM=196, BIAS=176, L=168, OT=172.5,
)
SLOT_AT = [168, 176, 184, 192, 128, 136, 152, 144]
GU_DONE = (3, 4, 7, 8)


def build(nc, x, win, wout, wg, wu, wd, bias, wsp, bsp, lng, lnb, gmix, ghead, gffn, gfin,
          tw, bd, onehot, mask, ident, out):
    ctx = ExitStack()
    with ctx:
        def at(name, kb, shape, dt=F32):
            return nc.alloc_sbuf_tensor_at(name, shape, dt, offset=BASE + int(kb * KB))

        X = at("x_res", AT["X"], [P, KT_D, S])
        HH = at("h_hi", AT["HH"], [P, KT_D, S], F32R)
        HL = at("h_lo", AT["HL"], [P, KT_D, S], F32R)
        QT = at("q_t", AT["Q"], [P, WA // P, S])
        KT = at("k_t", AT["K"], [P, WA // P, S])
        VN = at("v_tok", AT["VN"], [P, S // P, WA])
        UV = at("uv_tok", AT["UV"], [P, 2, S // P, WB])
        XC = at("xc_tok", AT["XC"], [P, S // P, WB])
        MB, MC = UV[:, 0], XC[:, :, :]
        BIAS = at("bias_rel", AT["BIAS"], [P, HA, BR, BC])
        SQB = at("mix_sq", AT["SQB"], [P, 2, 8, WB])
        XG = at("x_scaled", AT["XG"], [P, 2, HALF])
        SQ = at("x_sq", AT["SQ"], [P, 4, HALF])
        ACC = at("x_sq_sum", AT["ACC"], [P, 2, HALF])
        RM = at("rstd_mix", AT["RM"], [P, 2, HALF])
        RF = at("rstd_ffn", AT["RF"], [P, 2, HALF])
        Z = at("dft8", AT["Z"], [P, 8, WB])
        EO = at("dft8_even_odd", AT["EO"], [P, 8, WB])
        T = at("dft8_sums", AT["T"], [P, 4, WB])
        AB = at("dft_t", AT["AB"], [P, 2, 8, 256])
        VB = [at("v_band0", AT["VB0"], [P, 4, WA]), at("v_band1", AT["VB1"], [P, 4, WA])]
        TW = at("twiddle", AT["TW"], [P, 8, 2, 256])
        L = at("logits", AT["L"], [P, 3, NKEY])
        OT = at("att_tok", AT["OT"], [P, HA, DH])
        AH = at("act_hi", AT["AH"], [P, 2, S], F32R)
        AL = at("act_lo", AT["AL"], [P, 2, S], F32R)
        SIL = at("silu_g", AT["SIL"], [P, 2, HALF])
        TT = at("gated", AT["TT"], [P, 2, HALF])
        WH = [at(f"w_hi{s}", SLOT_AT[s], [P, 1024], F32R) for s in range(SLOTS)]
        WL = [at(f"w_lo{s}", SLOT_AT[s] + 4, [P, 1024], F32R) for s in range(SLOTS)]
        WR = [at(f"w_raw{s}", SLOT_AT[s] + 4, [P, 1024]) for s in range(SLOTS)]
        OUTS = at("out_t", AT["HH"], [P, KT_D, S])
        small = [200 * KB]

        def keep(name, shape, dt=F32):
            size = int(np.prod(shape[1:])) * (2 if dt == F16 else 4)
            t = nc.alloc_sbuf_tensor_at(name, shape, dt, offset=BASE + small[0])
            small[0] += -(-size // 32) * 32
            return t

        IDENT = keep("ident", [P, P])
        ONES = keep("ones", [P, P])
        ONEHOT = keep("onehot", [96, P], F16)
        shared = small[0]
        BD = keep("channel_dft", [P, 2, P])
        WSP = keep("w_spatial_t", [P, HB, P])
        LNG = keep("ln_g", [P, WB])
        LNB = keep("ln_b", [P, WB])
        PT = nc.alloc_sbuf_tensor_at("probs_t", [P, 2, NKEY], F32, offset=BASE + shared)
        MASK = nc.alloc_sbuf_tensor_at("mask", [96, 2, NKEY], F16, offset=BASE + shared + 2 * NKEY * 4)
        BSP = keep("b_spatial", [P, HB])
        GM = keep("g_mix", [P, KT_D])
        GH = keep("g_head", [P, KT_D])
        GF = keep("g_ffn", [P, KT_D])
        GO = keep("g_final", [P, KT_D])
        NHALF = keep("minus_half", [P, 32])
        EPS_T = keep("eps", [P, 1])
        RT = keep("rstd_tok", [P, 8])
        ST = keep("bn_stats", [P, 8, 6])
        MV = keep("mean_var", [P, 8, 2])
        LR = keep("ln_rstd", [P, 8])
        SS = keep("head_ss", [P, 32])
        SR = keep("head_rstd", [P, 32])
        NM = keep("minus_max", [P, 4])
        SUM = keep("exp_sum", [P, 2, HA])
        RS = keep("exp_sum_inv", [P, HA])
        assert BASE + small[0] <= 229368

        B = [ctx.enter_context(nc.psum_tensor(f"bank{i}", [P, HALF], F32)) for i in range(8)]

        def sem(name):
            return ctx.enter_context(nc.semaphore(name))

        x_landed = [sem(f"x_landed{k}") for k in range(KT_D)]
        const_landed = sem("const_landed")
        layer_landed, gm_landed = sem("layer_landed"), sem("gm_landed")
        tw_landed, mask_landed = sem("tw_landed"), sem("mask_landed")
        bias_landed = [sem("bias_landed0"), sem("bias_landed1")]
        vb_landed = [sem("vb_landed0"), sem("vb_landed1")]
        w_landed = [sem(f"w_landed{s}") for s in range(SLOTS)]
        w_hi = [sem(f"w_hi{s}") for s in range(SLOTS)]
        w_ready = [sem(f"w_ready{s}") for s in range(SLOTS)]
        w_used = [sem(f"w_used{s}") for s in range(SLOTS)]
        memsets = sem("memsets")
        dve_passed, sp_passed = sem("dve_passed"), sem("sp_passed")

        class Norm:

            def __init__(self, name):
                self.hi, self.lo, self.sq, self.acc, self.ssq, self.v, self.r = (
                    sem(f"{name}_{x}") for x in ("hi", "lo", "sq", "acc", "ssq", "v", "r"))

        n_mix, n_ffn, n_fin = Norm("nm"), Norm("nf"), Norm("no")
        xg_made, first_lo, acc_dve = sem("xg_made"), sem("first_lo"), sem("acc_dve")
        acc_full = sem("acc_full")
        rt_var, rt_made = sem("rt_var"), sem("rt_made")
        xc_act, xc_dve, z_ev, q_ev, k_ev, v_act, v_dve = (
            sem(x) for x in ("xc_act", "xc_dve", "z_ev", "q_ev", "k_ev", "v_act", "v_dve"))
        ln_stat, ln_var, ln_rstd, ln_step = sem("ln_stat"), sem("ln_var"), sem("ln_rstd"), sem("ln_step")
        sp_full, mb_made = sem("sp_full"), sem("mb_made")
        fft_step = sem("fft_step")
        dft_full, ab_act, ab_dve, cd_full, mc_made = (
            sem("dft_full"), sem("ab_act"), sem("ab_dve"), sem("cd_full"), sem("mc_made"))
        hs_sq, hs_red, hs_var, hs_rstd, hs_norm = (
            sem("hs_sq"), sem("hs_red"), sem("hs_var"), sem("hs_rstd"), sem("hs_norm"))
        bt_full, bt_hi, bt_lo = sem("bt_full"), sem("bt_hi"), sem("bt_lo")
        s_full, l_made, p_made, pt_full, pt_made, pv_done = (
            sem("s_full"), sem("l_made"), sem("p_made"), sem("pt_full"), sem("pt_made"), sem("pv_done"))
        o_inv, o_made, o_sq, o_red, o_var, o_rstd, o_norm = (
            sem("o_inv"), sem("o_made"), sem("o_sq"), sem("o_red"), sem("o_var"), sem("o_rstd"), sem("o_norm"))
        ot_full, ot_hi, ot_lo = sem("ot_full"), sem("ot_hi"), sem("ot_lo")
        out_full, out_added = sem("out_full"), sem("out_added")
        gate_read, up_read = sem("gate_read"), sem("up_read")
        gu_full, sil_made, gated, a_hi, a_lo, dn_full, dn_added = (
            sem("gu_full"), sem("sil_made"), sem("gated"), sem("a_hi"), sem("a_lo"), sem("dn_full"),
            sem("dn_added"))
        out_ready, out_pool, stored = sem("out_ready"), sem("out_pool"), sem("stored")
        out_scaled = sem("out_scaled")
        POOL_OUT = 7

        block = ctx.enter_context(nc.Block())

        def half(h):
            return slice(h * HALF, (h + 1) * HALF)

        def grid(ap):
            return ap.rearrange("p (r c) -> p r c", c=GW)

        K_MAJOR = [(k, h) for k in range(KT_D) for h in range(2)]
        H_MAJOR = [(k, h) for h in range(2) for k in range(KT_D)]
        MIX_HI = H_MAJOR[:2] + [(0, 1)] + H_MAJOR[2:8] + H_MAJOR[9:]
        FFN_LO = K_MAJOR[:8] + [(k, h) for h in range(2) for k in range(4, KT_D)]

        def at_k(k):
            return OUT_ORDER[k]

        def summed(order, i):
            k, h = order[i]
            first = [j for j, (_, hh) in enumerate(order) if hh == h][:2]
            last = max(i, first[1])
            return sum(order[j] != order[[hh for _, hh in order].index(order[j][1])] for j in range(last + 1))

        def x_ready(e, l, k, h):
            e.wait_ge(x_landed[k if k < 2 else k - k % 2], 16)
            e.wait_ge(dn_added, l * ADDS + (8 * h + k + 1 + ADD_CREDIT - 16))

        def qk_out(g, b):
            if g:
                return KT[:, b // 2, half(b % 2)]
            return QT[:, b // 2, :].rearrange("p (j h r c) -> p h r j c", j=NJ, h=2, c=QC)[:, b % 2]

        def qk_in(g, b):
            return B[b][:, :] if g else B[b][:, :].rearrange("p (r j c) -> p r j c", j=NJ, c=QC)

        def batch_out(t, b):
            k, q = 4 + b // 2, b % 2
            if b < 4:
                return t[:, k, half(q)]
            return t[:, k, :].rearrange("p (c a) -> p a c", a=8)[:, 4 * q:4 * q + 4, :]

        def batch_in(b):
            bank = B[6 + b % 2][:, :]
            return bank if b < 4 else bank.rearrange("p (a c) -> p a c", a=4)

        def tile_out(t, tile, k):
            j, rr = divmod(tile, 2)
            return grid(t[:, k, :])[:, QR * rr:QR * (rr + 1), QC * j:QC * (j + 1)]

        def tile_in(tile, k):
            return B[6 + tile % 2][:, k * P:(k + 1) * P].rearrange("p (r c) -> p r c", c=QC)

        def load_out(sp, l, p, slot_free):
            s = slot_free(OUT_P + p)
            g, kk = p // 4, OUT_ORDER[2 * (p % 4)]
            sp.dma_start(WR[s][:, :].rearrange("p (k n) -> p k n", k=2),
                         wout[l, kk:kk + 2, :, g * 512:(g + 1) * 512].rearrange("k p n -> p k n"))\
              .then_inc(w_landed[s], 16)

        @block.sync
        def _(sp):
            def passed():
                sp.sem_inc(sp_passed, 1)

            with sp.Fori(0, DEPTH) as l:
                def wait_released(p):
                    passed()
                    s = ALL_SLOT[p]
                    if p not in GROUP_END:
                        nth = sum(ALL_SLOT[o] == s and o not in GROUP_END for o in range(p + 1))
                        sp.wait_ge(w_used[s], l * USED[s] + nth)
                    elif p < 18:
                        sp.wait_ge(acc_full, l * 40 + GROUP_END[p])
                    else:
                        sp.wait_ge(out_full, l * 16 + GROUP_END[p])

                def slot_free(p):
                    before = [o for o in range(p) if ALL_SLOT[o] == ALL_SLOT[p]]
                    if before:
                        wait_released(before[-1])
                    elif ALL_SLOT[p] < 4:
                        sp.wait_ge(gu_full, l * (8 * NI) + (GU_CREDIT - 8 + GU_DONE[ALL_SLOT[p]]))
                    passed()
                    return ALL_SLOT[p]

                def load_piece(p):
                    s = slot_free(p)
                    g = max(n for n in range(5) if FIRST_P[n] <= p)
                    c0 = COLUMN[GROUPS[g]]
                    per = 2 if g else 4
                    kk = per * (p - FIRST_P[g])
                    sp.dma_start(WR[s][:, :].rearrange("p (k n) -> p k n", k=per),
                                 win[l, kk:kk + per, :, c0:c0 + 1024 // per].rearrange("k p n -> p k n"))\
                      .then_inc(w_landed[s], 16)

                sp.dma_start(GM[:, :], gmix[l]).then_inc(gm_landed, 16)
                load_piece(0)
                sp.dma_start(GH[:, :], ghead[l]).then_inc(layer_landed, 16)
                sp.dma_start(GF[:, :], gffn[l]).then_inc(layer_landed, 16)
                sp.dma_start(LNG[:, :], lng[l]).then_inc(layer_landed, 16)
                sp.dma_start(LNB[:, :], lnb[l]).then_inc(layer_landed, 16)
                sp.dma_start(BSP[:, :], bsp[l]).then_inc(layer_landed, 16)
                sp.dma_start(WSP[:, :, :], wsp[l]).then_inc(layer_landed, 16)
                sp.dma_start(BD[:, :, :], bd).then_inc(layer_landed, 16)
                sp.wait_ge(x_landed[KT_D - 2], 16)
                for p in (1, 2):
                    load_piece(p)
                sp.wait_ge(dn_full, l * (16 * NI) + DN_CREDIT)
                passed()
                sp.dma_start(TW[:, :, :, :], tw).then_inc(tw_landed, 16)
                for p in range(3, 14):
                    load_piece(p)
                sp.wait_ge(cd_full, l * 2 + 2)
                passed()
                sp.dma_start(MASK[:, :, :], mask).then_inc(mask_landed, 16)
                sp.wait_ge(sp_full, (l + 1) * HB)
                load_piece(14)
                load_piece(15)
                sp.wait_ge(k_ev, (l + 1) * 8)
                for n in range(2):
                    passed()
                    sp.dma_start(BIAS[:, 4 * n:4 * n + 4], bias[l, :, 4 * n:4 * n + 4]).then_inc(bias_landed[n], 16)
                    load_piece(16 + n)

                def load_rows(j, r):
                    p0 = (r % 2) * GW + BAND[j]
                    sp.dma_start(VB[j % 2][r * KC:(r + 1) * KC, :, :],
                                 VN[p0:p0 + KC, r // 2:S // P:2, :]).then_inc(vb_landed[j % 2], 16)

                sp.wait_ge(v_act, l * 4 + 4)
                load_rows(0, 0)
                load_rows(0, 1)
                sp.wait_ge(v_dve, l * 4 + 4)
                load_rows(0, 2)
                load_rows(0, 3)
                passed()
                sp.wait_ge(bt_full, l * 8 + 8)
                passed()
                for j in range(1, NJ):
                    if j >= 2:
                        sp.wait_ge(pv_done, l * 64 + 16 * (j - 1))
                        passed()
                    for r in range(4):
                        load_rows(j, r)
                    if j == 1:
                        load_out(sp, l, 0, slot_free)
                for j in (0, 1):
                    sp.wait_ge(vb_landed[j], (l + 1) * (2 * 4 * 16))
                    passed()
                for p in range(1, 8):
                    if p == 3:
                        sp.wait_ge(l_made, l * 64 + 64)
                        passed()
                    if p == 6:
                        sp.wait_ge(ot_full, l * 8 + 8)
                        passed()
                    load_out(sp, l, p, slot_free)
                with sp.Fori(0, NI) as i:
                    for s in range(6):
                        wait_released(LAST_P[s])
                        passed()
                        if s < 4:
                            sp.wait_ge(gu_full, (l * NI + i) * 8 + (GU_CREDIT - 8 + GU_DONE[s]))
                        else:
                            sp.wait_ge(dn_full, (l * NI + i) * 16 + DN_CREDIT)
                        passed()
                        src = (wg[l, 2 * i + s // 2] if s in (0, 2) else
                               wu[l, 2 * i + s // 2] if s in (1, 3) else wd[l, 2 * i + (s - 4)])
                        sp.dma_start(WR[s][:, :], src).then_inc(w_landed[s], 16)
            order = [POOL_OUT]
            for n in range(1, 9):
                order += [n - 1] * (n <= POOL_OUT) + [POOL_OUT + n]
            for i in order:
                k, h = H_MAJOR[i]
                if i < POOL_OUT:
                    sp.wait_ge(out_pool, i + 1)
                else:
                    sp.wait_ge(out_ready, i - POOL_OUT + 1)
                sp.dma_start(out[k, :, half(h)], OUTS[:, k, half(h)]).then_inc(stored, 16)
            sp.wait_ge(stored, 16 * 16)

        @block.gpsimd
        def _(pool):
            nc.gpsimd.memset(ONES[:, :], 1.0).then_inc(memsets, 1)
            nc.gpsimd.memset(NHALF[:, :], -0.5).then_inc(memsets, 1)
            nc.gpsimd.memset(EPS_T[:, :], EPS).then_inc(memsets, 1)
            pool.wait_ge(gm_landed, 16)
            for k in range(2, KT_D, 2):
                pool.dma_start(X[:, k:k + 2, :], x[k:k + 2].rearrange("k p n -> p k n"))\
                    .then_inc(x_landed[k], 16)
            for dst, src in ((ONEHOT, onehot), (GO, gfin), (IDENT, ident)):
                pool.dma_start(dst[:, :], src).then_inc(const_landed, 16)
            pool.wait_ge(memsets, 3)

            def split_lo(s, nth):
                pool.wait_ge(w_hi[s], nth)
                nc.gpsimd.tensor_tensor(WL[s][:, :], WR[s][:, :], WH[s][:, :], ALU.subtract)\
                    .then_inc(w_ready[s], 1)

            def sum_squares(n, l, order, tiles, per=14):
                for i in tiles:
                    k, h = order[i]
                    if k == 0:
                        continue
                    pool.wait_ge(n.sq, l * 16 + i + 1)
                    done = summed(order, i) - 1
                    if k > 1:
                        pool.wait_ge(n.acc, l * per + done)
                        nc.gpsimd.tensor_tensor(ACC[:, h, :], ACC[:, h, :], SQ[:, i % 4, :], ALU.add)\
                            .then_inc(n.acc, 1)
                    else:
                        i0 = order.index((0, h))
                        nc.gpsimd.tensor_tensor(ACC[:, h, :], SQ[:, i0 % 4, :], SQ[:, i % 4, :], ALU.add)\
                            .then_inc(n.acc, 1)

            with pool.Fori(0, DEPTH) as l:
                def piece_lo(p):
                    s = ALL_SLOT[p]
                    split_lo(s, l * PER_SLOT[s] + (nth_in_slot(p) + 1))

                def ffn_lo(s, i):
                    split_lo(s, l * PER_SLOT[s] + i + (FFN_FIRST[s] + 1))

                piece_lo(0)
                for h in range(2):
                    pool.wait_ge(xg_made, l * 2 + h + 1)
                    nc.gpsimd.tensor_tensor(HL[:, 0, half(h)], XG[:, h, :], HH[:, 0, half(h)], ALU.subtract)\
                        .then_inc(first_lo, 1)
                sum_squares(n_mix, l, H_MAJOR, range(4), 7)
                piece_lo(1)
                sum_squares(n_mix, l, H_MAJOR, range(4, 8), 7)
                piece_lo(2)
                pool.wait_ge(rt_var, l + 1)
                nc.gpsimd.tensor_tensor(RT[:, :], RT[:, :], NHALF[:, 0:8], ALU.pow).then_inc(rt_made, 1)
                for p in range(3, 9):
                    piece_lo(p)
                pool.wait_ge(ln_var, l + 1)
                nc.gpsimd.tensor_tensor(LR[:, :], LR[:, :], NHALF[:, 0:8], ALU.pow).then_inc(ln_rstd, 1)
                for p in range(9, 14):
                    piece_lo(p)
                for n in range(2):
                    pool.wait_ge(hs_var, l * 2 + n + 1)
                    nc.gpsimd.tensor_tensor(SR[:, :], SS[:, :], NHALF[:, :], ALU.pow).then_inc(hs_rstd, 1)
                for p in range(14, 18):
                    piece_lo(p)
                for t in range(8):
                    pool.wait_ge(o_var, l * 8 + t + 1)
                    nc.gpsimd.tensor_tensor(SR[:, 0:HA], SS[:, 0:HA], NHALF[:, 0:HA], ALU.pow).then_inc(o_rstd, 1)
                    if t in (3, 6):
                        for p in {3: (0,), 6: (1, 2)}[t]:
                            piece_lo(OUT_P + p)
                for p in range(3, 8):
                    piece_lo(OUT_P + p)
                sum_squares(n_ffn, l, K_MAJOR, range(8))
                ffn_lo(0, 0)
                ffn_lo(1, 0)
                sum_squares(n_ffn, l, K_MAJOR, range(8, 16))
                for s in range(2, 6):
                    ffn_lo(s, 0)
                with pool.Fori(1, NI) as i:
                    for s in range(6):
                        ffn_lo(s, i)
            sum_squares(n_fin, 0, H_MAJOR, range(16))
            pool.wait_ge(n_fin.r, 1)
            for i, (k, h) in enumerate(H_MAJOR[:POOL_OUT]):
                pool.wait_ge(out_scaled, i + 1)
                nc.gpsimd.tensor_tensor(OUTS[:, k, half(h)], OUTS[:, k, half(h)], RF[:, h, :], ALU.mult)\
                    .then_inc(out_pool, 1)

        @block.scalar
        def _(act):
            for k in range(2):
                act.dma_start(X[:, k, :], x[k]).then_inc(x_landed[k], 16)
            act.sem_inc(a_hi, SPLIT_CREDIT)
            act.wait_ge(memsets, 3)

            def x_hi(n, k, h, g, slot):
                nc.scalar.activation(HH[:, slot, half(h)], X[:, k, half(h)], ACT.Copy,
                                     scale=g[:, k:k + 1]).then_inc(n.hi, 1)

            def x_square(n, l, order, i):
                k, h = order[i]
                if i >= 4:
                    if n is not n_mix:
                        act.wait_ge(n.acc, l * 14 + summed(order, i - 4))
                    elif i < 12:
                        act.wait_ge(n.acc, l * 7 + summed(order, i - 4))
                    else:
                        act.wait_ge(acc_dve, l * 7 + summed(order, i - 4) - 7)
                nc.scalar.activation(SQ[:, i % 4, :], X[:, k, half(h)], ACT.Square).then_inc(n.sq, 1)

            def rms(n, l, to, per):
                for h in range(2):
                    act.wait_ge(n.ssq, l * per + h + 1)
                    nc.scalar.activation(to[:, h, :], B[4 + h][:, :], ACT.Sqrt, scale=1.0 / D,
                                         bias=EPS_T[:, :]).then_inc(n.v, 1)

            def split_hi(s, nth):
                act.wait_ge(w_landed[s], nth * 16)
                nc.scalar.activation(WH[s][:, :], WR[s][:, :], ACT.Copy).then_inc(w_hi[s], 1)

            with act.Fori(0, DEPTH) as l:
                def piece_hi(p):
                    s = ALL_SLOT[p]
                    split_hi(s, l * PER_SLOT[s] + (nth_in_slot(p) + 1))

                act.wait_ge(gm_landed, (l + 1) * 16)
                for i, (k, h) in enumerate(MIX_HI):
                    x_ready(act, l, k, h)
                    x_hi(n_mix, k, h, GM, k)
                    if i == 2:
                        piece_hi(0)
                        for q in range(2):
                            nc.scalar.activation(XG[:, q, :], X[:, 0, half(q)], ACT.Copy,
                                                 scale=GM[:, 0:1]).then_inc(xg_made, 1)
                    if i >= 9:
                        x_square(n_mix, l, H_MAJOR, i - 9)
                    if i == 12:
                        piece_hi(1)
                x_square(n_mix, l, H_MAJOR, 7)
                for i in range(8, 12):
                    x_square(n_mix, l, H_MAJOR, i)
                piece_hi(2)
                for i in range(12, 16):
                    x_square(n_mix, l, H_MAJOR, i)
                rms(n_mix, l, RM, 3)
                act.wait_ge(layer_landed, (l + 1) * (7 * 16))
                act.wait_ge(rt_made, l + 1)
                for b in (0, 1, 4, 5):
                    act.wait_ge(acc_full, l * 40 + (b | 1) + 1)
                    nc.scalar.activation(XC[:, b, :], B[b // 2][:, (b % 2) * WB:(b % 2 + 1) * WB], ACT.Copy,
                                         scale=RT[:, b:b + 1]).then_inc(xc_act, 1)
                for p in range(3, 8):
                    piece_hi(p)
                for n, b in enumerate(BANKS):
                    act.wait_ge(acc_full, l * 40 + 8 + n + 1)
                    nc.scalar.activation(UV[:, :, b, :], B[b][:, :].rearrange("p (u n) -> p u n", u=2),
                                         ACT.Gelu_apprx_tanh, scale=RT[:, b:b + 1]).then_inc(z_ev, 1)
                for b in range(4):
                    act.wait_ge(dft_full, l * 8 + b + 1)
                    nc.scalar.activation(AB[:, 0, 2 * b:2 * b + 2, :], B[4 + b][:, :], ACT.Copy).then_inc(ab_act, 1)
                for p in range(8, 12):
                    piece_hi(p)
                act.wait_ge(cd_full, l * 2 + 2)
                for b in range(4):
                    nc.scalar.activation(MC[:, 2 * b:2 * b + 2, :], B[b][:, :].rearrange("p (a n) -> p a n", a=2),
                                         ACT.Copy).then_inc(mc_made, 1)
                piece_hi(12)
                act.wait_ge(mb_made, l * 4 + 4)
                nc.scalar.activation(SQB[:, 0], MB, ACT.Square).then_inc(hs_sq, 1)
                act.wait_ge(mc_made, l * 4 + 4)
                nc.scalar.activation(SQB[:, 1], MC, ACT.Square).then_inc(hs_sq, 1)
                for p in range(13, 18):
                    piece_hi(p)
                for n, b in enumerate(BANKS):
                    if b % 2 == 0:
                        act.wait_ge(acc_full, l * 40 + 32 + n + 1)
                        nc.scalar.activation(VN[:, b, :], B[b][:, :], ACT.Copy,
                                             scale=RT[:, b:b + 1]).then_inc(v_act, 1)

                for t in range(73):
                    if t < 64:
                        act.wait_ge(l_made, l * 64 + t + 1)
                        if t >= 16 and t % 8 == 0:
                            act.wait_ge(o_inv, l * 8 + t // 8 - 1)
                        nc.scalar.activation(L[:, t % 3, :], L[:, t % 3, :], ACT.Exp, scale=-1.0,
                                             bias=NM[:, t % 4:t % 4 + 1],
                                             accum_out=SUM[:, (t // 8) % 2, t % 8:t % 8 + 1]).then_inc(p_made, 1)
                    if t in (36, 60):
                        for p in {36: (0,), 60: (1, 2)}[t]:
                            piece_hi(OUT_P + p)
                    if t < 8:
                        k = 4 + t // 2
                        act.wait_ge(bt_full, l * 8 + t + 1)
                        nc.scalar.activation(batch_out(HH, t), batch_in(t), ACT.Copy,
                                             scale=GH[:, k:k + 1]).then_inc(bt_hi, 1)
                    tile, ph = divmod(t - 9, 8)
                    if t >= 11 and ph == 2:
                        act.wait_ge(o_made, l * 8 + tile + 1)
                        if tile < 2:
                            act.wait_ge(bt_lo, l * 8 + 7 + tile)
                        else:
                            act.wait_ge(ot_lo, l * 32 + 4 * (tile - 1))
                        nc.scalar.activation(B[6 + tile % 2][:, :].rearrange("p (h d) -> p h d", d=DH), OT[:, :, :],
                                             ACT.Square).then_inc(o_sq, 1)
                    if t >= 15 and ph == 6:
                        act.wait_ge(ot_full, l * 8 + tile + 1)
                        for k in range(4):
                            nc.scalar.activation(tile_out(HH, tile, k), tile_in(tile, k), ACT.Copy,
                                                 scale=GH[:, k:k + 1]).then_inc(ot_hi, 1)

                for p in range(3, 8):
                    piece_hi(OUT_P + p)
                for i, (k, h) in enumerate(K_MAJOR):
                    if h == 0 and k in (0, 2):
                        q = OUT_P + 4 + k // 2
                        s = ALL_SLOT[q]
                        act.wait_ge(w_used[s], l * USED[s] + sum(
                            ALL_SLOT[o] == s and o not in GROUP_END for o in range(q + 1)))
                    act.wait_ge(out_added, l * 16 + i + 1)
                    x_hi(n_ffn, k, h, GF, at_k(k))
                    if k < 4:
                        x_square(n_ffn, l, K_MAJOR, i)
                    if i == 7:
                        split_hi(0, l * PER_SLOT[0] + (FFN_FIRST[0] + 1))
                        split_hi(1, l * PER_SLOT[1] + (FFN_FIRST[1] + 1))
                for i in range(8, 16):
                    x_square(n_ffn, l, K_MAJOR, i)
                split_hi(2, l * PER_SLOT[2] + (FFN_FIRST[2] + 1))
                split_hi(3, l * PER_SLOT[3] + (FFN_FIRST[3] + 1))
                rms(n_ffn, l, RF, 2)

                def turn(i):
                    F = (l * NI + i) * 4

                    def silu(f, h):
                        act.wait_ge(gate_read, F + (2 * f + h + 1 + GATE_CREDIT))
                        nc.scalar.activation(SIL[:, h, :], SIL[:, h, :], ACT.Silu).then_inc(sil_made, 1)

                    def gated_hi(f, h):
                        act.wait_ge(gated, F + (2 * f + h + 1 + GATED_CREDIT))
                        nc.scalar.activation(AH[:, f, half(h)], TT[:, h, :], ACT.Copy).then_inc(a_hi, 1)

                    silu(0, 0)
                    split_hi(4, l * PER_SLOT[4] + i + (FFN_FIRST[4] + 1))
                    gated_hi(0, 0)
                    silu(0, 1)
                    split_hi(5, l * PER_SLOT[5] + i + (FFN_FIRST[5] + 1))
                    gated_hi(0, 1)
                    for h in range(2):
                        silu(1, h)
                        gated_hi(1, h)

                turn(0)
                with act.Fori(1, NI) as i:
                    for s in range(4):
                        split_hi(s, l * PER_SLOT[s] + i + (FFN_FIRST[s] + 1))
                    turn(i)
            act.wait_ge(const_landed, 3 * 16)

            def scale_out(k, h):
                nc.scalar.activation(OUTS[:, k, half(h)], X[:, k, half(h)], ACT.Copy,
                                     scale=GO[:, k:k + 1]).then_inc(out_scaled, 1)

            for i, (k, h) in enumerate(H_MAJOR):
                act.wait_ge(dn_added, DEPTH * ADDS + ADD_CREDIT - 16 + i + 1)
                x_square(n_fin, 0, H_MAJOR, i)
                if 8 <= i < 15:
                    scale_out(i - 8, 0)
            rms(n_fin, 0, RF, 2)
            for k, h in H_MAJOR[7:]:
                scale_out(k, h)

        @block.vector
        def _(dve):
            dve.sem_inc(gated, GATED_CREDIT)
            dve.sem_inc(gate_read, GATE_CREDIT)
            dve.sem_inc(up_read, UP_CREDIT)
            dve.sem_inc(a_lo, SPLIT_CREDIT)
            dve.sem_inc(dn_added, ADD_CREDIT)

            def invert(n, l, r):
                for h in range(2):
                    dve.wait_ge(n.v, l * 2 + h + 1)
                    nc.vector.reciprocal(r[:, h, :], r[:, h, :]).then_inc(n.r, 1)

            def x_lo(n, k, h, g, slot):
                nc.vector.scalar_tensor_tensor(out=HL[:, slot, half(h)], in0=X[:, k, half(h)], scalar=g[:, k:k + 1],
                                               in1=HH[:, slot, half(h)], op0=ALU.mult, op1=ALU.subtract)\
                    .then_inc(n.lo, 1)

            with dve.Fori(0, DEPTH) as l:
                dve.wait_ge(gm_landed, (l + 1) * 16)
                for k, h in K_MAJOR[2:]:
                    dve.wait_ge(n_mix.hi, l * 16 + MIX_HI.index((k, h)) + 1)
                    x_lo(n_mix, k, h, GM, k)
                for k in range(1, KT_D):
                    dve.wait_ge(n_mix.sq, l * 16 + 8 + k + 1)
                    if k > 1:
                        dve.wait_ge(acc_dve, l * 7 + k - 1)
                    nc.vector.tensor_tensor(ACC[:, 1, :], ACC[:, 1, :] if k > 1 else SQ[:, 0, :], SQ[:, k % 4, :],
                                            ALU.add).then_inc(acc_dve, 1)
                dve.wait_ge(layer_landed, (l + 1) * (7 * 16))
                dve.wait_ge(n_mix.ssq, l * 3 + 3)
                nc.vector.tensor_scalar(RT[:, :], B[6][:, 0:8], 1.0 / D, EPS, ALU.mult, ALU.add).then_inc(rt_var, 1)
                dve.wait_ge(rt_made, l + 1)
                for b in (2, 3, 6, 7):
                    dve.wait_ge(acc_full, l * 40 + (b | 1) + 1)
                    nc.vector.tensor_scalar(XC[:, b, :], B[b // 2][:, (b % 2) * WB:(b % 2 + 1) * WB], RT[:, b:b + 1],
                                            None, ALU.mult).then_inc(xc_dve, 1)

                step = [0]

                def fft(ins, wait=False):
                    ins.then_inc(fft_step, 1)
                    step[0] += 1
                    if wait:
                        dve.wait_ge(fft_step, l * FFT_STEPS + step[0])

                dve.wait_ge(xc_act, (l + 1) * 4)
                dve.wait_ge(xc_dve, (l + 1) * 4)
                fft(nc.vector.tensor_tensor(EO[:, 0:4, :], XC[:, 0:4, :], XC[:, 4:8, :], ALU.add))
                fft(nc.vector.tensor_tensor(EO[:, 4:8, :], XC[:, 0:4, :], XC[:, 4:8, :], ALU.subtract), True)
                fft(nc.vector.tensor_tensor(T[:, 0:2, :], EO[:, 0:2, :], EO[:, 2:4, :], ALU.add))
                fft(nc.vector.tensor_tensor(T[:, 2, :], EO[:, 5, :], EO[:, 7, :], ALU.subtract))
                fft(nc.vector.tensor_tensor(T[:, 3, :], EO[:, 5, :], EO[:, 7, :], ALU.add))
                fft(nc.vector.tensor_tensor(Z[:, 2, :], EO[:, 0, :], EO[:, 2, :], ALU.subtract))
                fft(nc.vector.tensor_tensor(Z[:, 6, :], EO[:, 3, :], EO[:, 1, :], ALU.subtract), True)
                fft(nc.vector.tensor_tensor(Z[:, 0, :], T[:, 0, :], T[:, 1, :], ALU.add))
                fft(nc.vector.tensor_tensor(Z[:, 4, :], T[:, 0, :], T[:, 1, :], ALU.subtract))
                c = 0.5 ** 0.5
                for z, t, s, o, op in ((1, 2, c, 4, ALU.add), (3, 2, -c, 4, ALU.add),
                                       (5, 3, -c, 6, ALU.subtract), (7, 3, -c, 6, ALU.add)):
                    fft(nc.vector.scalar_tensor_tensor(out=Z[:, z, :], in0=T[:, t, :], scalar=s, in1=EO[:, o, :],
                                                       op0=ALU.mult, op1=op))
                assert step[0] == FFT_STEPS

                invert(n_mix, l, RM)

                for n, b in enumerate(BANKS):
                    dve.wait_ge(z_ev, l * 8 + n + 1)
                    nc.vector.bn_stats(ST[:, b, :], UV[:, 1, b, :]).then_inc(ln_stat, 1)
                    dve.wait_ge(ln_stat, l * 16 + 2 * n + 1)
                    dve.sem_inc(dve_passed, 1)
                    nc.vector.bn_aggr(MV[:, b, :], ST[:, b, :]).then_inc(ln_stat, 1)
                dve.wait_ge(ln_stat, l * 16 + 16)
                nc.vector.tensor_scalar(LR[:, :], MV[:, :, 1], EPS, None, ALU.add).then_inc(ln_var, 1)
                for b in range(4):
                    dve.wait_ge(dft_full, l * 8 + 4 + b + 1)
                    nc.vector.tensor_copy(AB[:, 1, 2 * b:2 * b + 2, :],
                                          B[b][:, :].rearrange("p (a n) -> p a n", a=2)).then_inc(ab_dve, 1)
                dve.wait_ge(ln_rstd, l + 1)
                for b in range(8):
                    nc.vector.tensor_scalar(UV[:, 1, b, :], UV[:, 1, b, :], MV[:, b, 0:1], LR[:, b:b + 1],
                                            ALU.subtract, ALU.mult).then_inc(ln_step, 1)
                dve.wait_ge(ln_step, l * 10 + 8)
                nc.vector.tensor_tensor(UV[:, 1], UV[:, 1],
                                        LNG[:, :].rearrange("p (a n) -> p a n", a=1).to_broadcast([P, 8, WB]),
                                        ALU.mult).then_inc(ln_step, 1)
                dve.wait_ge(ln_step, l * 10 + 9)
                nc.vector.tensor_tensor(UV[:, 1], UV[:, 1],
                                        LNB[:, :].rearrange("p (a n) -> p a n", a=1).to_broadcast([P, 8, WB]),
                                        ALU.add).then_inc(ln_step, 1)

                def qk_evacuate(g, done):
                    dve.wait_ge(n_mix.r, l * 2 + 2)
                    for n, b in enumerate(BANKS):
                        dve.wait_ge(acc_full, l * 40 + 16 + 8 * g + n + 1)
                        r = RM[:, b % 2, :]
                        if g:
                            nc.vector.scalar_tensor_tensor(out=qk_out(g, b), in0=qk_in(g, b), scalar=DH ** -0.5,
                                                           in1=r, op0=ALU.mult, op1=ALU.mult).then_inc(done, 1)
                        else:
                            nc.vector.tensor_tensor(qk_out(g, b), qk_in(g, b),
                                                    r.rearrange("p (r j c) -> p r j c", j=NJ, c=QC),
                                                    ALU.mult).then_inc(done, 1)

                qk_evacuate(0, q_ev)
                for h in range(HB):
                    dve.wait_ge(sp_full, l * HB + h + 1)
                    u = UV[:, 0, :, h * DH:(h + 1) * DH]
                    nc.vector.scalar_tensor_tensor(
                        out=u, in0=B[4 + h][:, :].rearrange("p (n d) -> p n d", d=DH), scalar=BSP[:, h:h + 1],
                        in1=u, op0=ALU.add, op1=ALU.mult).then_inc(mb_made, 1)

                def head_norm(n, m, sq):
                    dve.wait_ge(hs_sq, l * 2 + n + 1)
                    if n:
                        dve.wait_ge(hs_rstd, l * 2 + n)
                    nc.vector.tensor_reduce(SS[:, :], sq, AX_X, ALU.add).then_inc(hs_red, 1)
                    dve.wait_ge(hs_red, l * 2 + n + 1)
                    nc.vector.tensor_scalar(SS[:, :], SS[:, :], 1.0 / DH, EPS, ALU.mult, ALU.add).then_inc(hs_var, 1)

                def head_scale(n, m):
                    dve.wait_ge(hs_rstd, l * 2 + n + 1)
                    v = m.rearrange("p n (h d) -> p (n h) d", d=DH)
                    nc.vector.tensor_tensor(v, v, SR[:, :].rearrange("p (g a) -> p g a", a=1)
                                            .to_broadcast([P, 32, DH]), ALU.mult).then_inc(hs_norm, 1)

                for n, m in enumerate((MB, MC)):
                    head_norm(n, m, SQB[:, n].rearrange("p n (h d) -> p (n h) d", d=DH))
                    head_scale(n, m)
                qk_evacuate(1, k_ev)
                for n, b in enumerate(BANKS):
                    if b % 2:
                        dve.wait_ge(acc_full, l * 40 + 32 + n + 1)
                        nc.vector.tensor_scalar(VN[:, b, :], B[b][:, :], RT[:, b:b + 1], None,
                                                ALU.mult).then_inc(v_dve, 1)

                for t in range(73):
                    if t in (0, 4):
                        dve.wait_ge(bias_landed[t // 4], (l + 1) * 16)
                    if t < 64:
                        j, rr, h = t // 16, (t // 8) % 2, t % 8
                        dve.wait_ge(s_full, l * 64 + t + 1)
                        if t >= 3:
                            dve.wait_ge(pt_full, l * 64 + t - 2)
                        dve.sem_inc(dve_passed, 1)
                        r0, c0 = 4 * (1 - rr), BCOL[j]
                        nc.vector.tensor_tensor_reduce(
                            L[:, t % 3, :].rearrange("p (r c) -> p r c", c=KC),
                            B[t % 2][:, 0:NKEY].rearrange("p (r c) -> p r c", c=KC),
                            BIAS[:, h, r0:r0 + KR, c0:c0 + KC], -1.0, 3e38, ALU.add, ALU.min,
                            NM[:, t % 4:t % 4 + 1]).then_inc(l_made, 1)
                    if 2 <= t <= 65:
                        u = t - 2
                        dve.wait_ge(pt_full, l * 64 + u + 1)
                        if u >= 2:
                            dve.wait_ge(pv_done, l * 64 + u - 1)
                        nc.vector.tensor_copy(PT[:, u % 2, :], B[2 + u % 2][:, 0:NKEY]).then_inc(pt_made, 1)
                    if 1 <= t <= 8:
                        b = t - 1
                        k = 4 + b // 2
                        dve.wait_ge(bt_hi, l * 8 + b + 1)
                        nc.vector.scalar_tensor_tensor(out=batch_out(HL, b), in0=batch_in(b), scalar=GH[:, k:k + 1],
                                                       in1=batch_out(HH, b), op0=ALU.mult,
                                                       op1=ALU.subtract).then_inc(bt_lo, 1)
                    tile, ph = divmod(t - 9, 8)
                    if t >= 11 and ph == 2:
                        dve.wait_ge(p_made, l * 64 + 8 * tile + 8)
                        nc.vector.reciprocal(RS[:, :], SUM[:, tile % 2, :]).then_inc(o_inv, 1)
                        dve.wait_ge(o_inv, l * 8 + tile + 1)
                        dve.wait_ge(pv_done, l * 64 + 8 * tile + 8)
                        if tile:
                            dve.wait_ge(ot_full, l * 8 + tile)
                        nc.vector.tensor_tensor(OT[:, :, :], B[4 + tile % 2][:, :].rearrange("p (h d) -> p h d", d=DH),
                                                RS[:, :].rearrange("p (h a) -> p h a", a=1).to_broadcast([P, HA, DH]),
                                                ALU.mult).then_inc(o_made, 1)
                    if t >= 12 and ph == 3:
                        if tile:
                            dve.wait_ge(o_norm, l * 8 + tile)
                        else:
                            dve.wait_ge(hs_norm, l * 2 + 2)
                        dve.wait_ge(o_sq, l * 8 + tile + 1)
                        nc.vector.tensor_reduce(SS[:, 0:HA], B[6 + tile % 2][:, :].rearrange("p (h d) -> p h d", d=DH),
                                                AX_X, ALU.add).then_inc(o_red, 1)
                        dve.wait_ge(o_red, l * 8 + tile + 1)
                        nc.vector.tensor_scalar(SS[:, 0:HA], SS[:, 0:HA], 1.0 / DH, EPS, ALU.mult,
                                                ALU.add).then_inc(o_var, 1)
                    if t >= 14 and ph == 5:
                        dve.wait_ge(o_rstd, l * 8 + tile + 1)
                        nc.vector.tensor_tensor(OT[:, :, :], OT[:, :, :],
                                                SR[:, 0:HA].rearrange("p (h a) -> p h a", a=1)
                                                .to_broadcast([P, HA, DH]), ALU.mult).then_inc(o_norm, 1)
                    if t >= 16 and ph == 7:
                        for k in range(4):
                            dve.wait_ge(ot_hi, l * 32 + 4 * tile + 4)
                            nc.vector.scalar_tensor_tensor(out=tile_out(HL, tile, k), in0=tile_in(tile, k),
                                                           scalar=GH[:, k:k + 1], in1=tile_out(HH, tile, k),
                                                           op0=ALU.mult, op1=ALU.subtract).then_inc(ot_lo, 1)
                def add_out(b16):
                    k, h = divmod(b16, 2)
                    dve.wait_ge(out_full, l * 16 + b16 + 1)
                    nc.vector.tensor_tensor(X[:, k, half(h)], B[b16 % 8][:, :], X[:, k, half(h)],
                                            ALU.add).then_inc(out_added, 1)

                def ffn_x_lo(i):
                    k, h = FFN_LO[i]
                    dve.wait_ge(n_ffn.hi, l * 16 + K_MAJOR.index((k, h)) + 1)
                    x_lo(n_ffn, k, h, GF, at_k(k))

                for b in range(8):
                    add_out(b)
                for i in range(8):
                    ffn_x_lo(i)
                for b in range(8):
                    add_out(8 + b)
                    if b % 2 and b >= 3:
                        ffn_x_lo(8 + (b - 3) // 2)
                for i in range(11, 16):
                    ffn_x_lo(i)
                invert(n_ffn, l, RF)
                dve.wait_ge(n_ffn.r, l * 2 + 2)
                dve.sem_inc(dve_passed, 1)
                with dve.Fori(0, NI) as i:
                    F = (l * NI + i) * 4
                    for f in range(2):
                        for h in range(2):
                            n = 2 * f + h
                            dve.wait_ge(gu_full, (l * NI + i) * 8 + (4 * f + 2 * h + 1 + GU_CREDIT))
                            dve.wait_ge(gated, F + (n - 1 + GATED_CREDIT))
                            nc.vector.tensor_tensor(SIL[:, h, :], B[h][:, :], RF[:, h, :], ALU.mult)\
                                .then_inc(gate_read, 1)
                            dve.wait_ge(gu_full, (l * NI + i) * 8 + (4 * f + 2 * h + 2 + GU_CREDIT))
                            dve.wait_ge(a_hi, F + (n - 1 + SPLIT_CREDIT))
                            dve.wait_ge(a_lo, F + (n - 1 + SPLIT_CREDIT))
                            nc.vector.tensor_tensor(TT[:, h, :], B[2 + h][:, :], RF[:, h, :], ALU.mult)\
                                .then_inc(up_read, 1)
                            dve.wait_ge(up_read, F + (n + 1 + UP_CREDIT))
                            dve.wait_ge(sil_made, F + (n + 1))
                            nc.vector.tensor_tensor(TT[:, h, :], TT[:, h, :], SIL[:, h, :], ALU.mult)\
                                .then_inc(gated, 1)
                            dve.wait_ge(a_hi, F + (n + 1 + SPLIT_CREDIT))
                            nc.vector.tensor_tensor(AL[:, f, half(h)], TT[:, h, :], AH[:, f, half(h)], ALU.subtract)\
                                .then_inc(a_lo, 1)
                    for n in range(16):
                        h, k = divmod(n, 8)
                        dve.wait_ge(dn_full, (l * NI + i) * 16 + (n + 1 + DN_CREDIT))
                        nc.vector.tensor_tensor(X[:, k, half(h)], B[4 + n % 4][:, :], X[:, k, half(h)], ALU.add)\
                            .then_inc(dn_added, 1)
            invert(n_fin, 0, RF)
            dve.wait_ge(n_fin.r, 2)
            for k, h in H_MAJOR[POOL_OUT:]:
                dve.wait_ge(out_scaled, H_MAJOR.index((k, h)) + 1)
                nc.vector.tensor_tensor(OUTS[:, k, half(h)], OUTS[:, k, half(h)], RF[:, h, :], ALU.mult)\
                    .then_inc(out_ready, 1)

        @block.tensor
        def _(pe):
            pe.sem_inc(gu_full, GU_CREDIT)
            pe.sem_inc(dn_full, DN_CREDIT)
            pe.wait_ge(memsets, 3)

            def sum_features(n, l, h):
                if n is n_mix:
                    pe.wait_ge(acc_dve if h else n.acc, (l + 1) * 7)
                else:
                    pe.wait_ge(n.acc, l * 14 + (13 + h if n is n_ffn else 7 * (h + 1)))
                nc.tensor.matmul(B[4 + h][:, :], ONES[:, :], ACC[:, h, :], start=True, stop=True)\
                    .then_inc(n.ssq, 1)

            def split3(bank, lh, ll, rh, rl, start, stop):
                nc.tensor.matmul(bank, lh, rh, start=start, stop=False)
                nc.tensor.matmul(bank, lh, rl, start=False, stop=False)
                return nc.tensor.matmul(bank, ll, rh, start=False, stop=stop)

            with pe.Fori(0, DEPTH) as l:
                def wait_piece(p):
                    s = ALL_SLOT[p]
                    pe.wait_ge(w_ready[s], l * PER_SLOT[s] + (nth_in_slot(p) + 1))
                    return s

                def piece_done(p, mm):
                    if p not in GROUP_END:
                        mm.then_inc(w_used[ALL_SLOT[p]], 1)

                for k in range(KT_D):
                    p = k // 4
                    s = wait_piece(p) if k % 4 == 0 else ALL_SLOT[p]
                    w = slice(k % 4 * WB, (k % 4 + 1) * WB)
                    if k == KT_D - 1:
                        sum_features(n_mix, l, 0)
                        sum_features(n_mix, l, 1)
                        for b in range(8):
                            mm = nc.tensor.matmul(B[6][:, b:b + 1], ACC[:, b // 4, (b % 4) * P:(b % 4 + 1) * P],
                                                  ONES[:, 0:1], start=True, stop=True)
                        mm.then_inc(n_mix.ssq, 1)
                    if k:
                        pe.wait_ge(n_mix.lo, l * 14 + 2 * k)
                    else:
                        pe.wait_ge(first_lo, l * 2 + 2)
                    for b in range(8):
                        m = slice(b * P, (b + 1) * P)
                        mm = split3(B[b // 2][:, (b % 2) * WB:(b % 2 + 1) * WB], HH[:, k, m], HL[:, k, m],
                                    WH[s][:, w], WL[s][:, w], k == 0 and b % 2 == 0, k == KT_D - 1 and b % 2 == 1)
                        if k == KT_D - 1:
                            mm.then_inc(acc_full, 1)
                    if k == 3:
                        piece_done(p, mm)

                def project(g, bank_free):
                    for k in range(KT_D):
                        p = FIRST_P[g] + k // 2
                        s = wait_piece(p) if k % 2 == 0 else ALL_SLOT[p]
                        w = slice(k % 2 * 512, (k % 2 + 1) * 512)
                        wh, wl = WH[s][:, w], WL[s][:, w]
                        for n, b in enumerate(BANKS):
                            if k == 0:
                                bank_free(n, b)
                            if GROUPS[g] in "qk":
                                m, h = slice(b // 2 * P, (b // 2 + 1) * P), half(b % 2)
                                mm = split3(B[b][:, :], wh[:, m], wl[:, m], HH[:, k, h], HL[:, k, h],
                                            k == 0, k == KT_D - 1)
                            else:
                                m = slice(b * P, (b + 1) * P)
                                mm = split3(B[b][:, :], HH[:, k, m], HL[:, k, m], wh, wl, k == 0, k == KT_D - 1)
                            if k == KT_D - 1:
                                mm.then_inc(acc_full, 1)
                        if k % 2:
                            piece_done(p, mm)

                def after_xc(n, b):
                    if b in (4, 5):
                        pe.wait_ge(n_mix.v, l * 2 + b - 3)
                    elif b == 6:
                        pe.wait_ge(rt_var, l + 1)
                    elif b < 4:
                        pe.wait_ge(xc_dve if b % 2 else xc_act, l * 4 + 2 * (b // 2) + 2)

                project(1, after_xc)
                def position_dft(f, banks):
                    m = slice(f * P, (f + 1) * P)
                    for a in range(8):
                        bank = B[banks + a // 2][:, (a % 2) * 256:(a % 2 + 1) * 256]
                        zr, zi = min(a, 8 - a), 4 + min(a, 8 - a)
                        both = a not in (0, 4)
                        mm = nc.tensor.matmul(bank, Z[:, zr, m], TW[:, a, 0, :], start=True, stop=not both)
                        if both:
                            mm = nc.tensor.matmul(bank, Z[:, zi, m], TW[:, a, 1, :], start=False, stop=True)
                        if a % 2:
                            mm.then_inc(dft_full, 1)

                def channel_dft(f):
                    for a in range(8):
                        bank = B[a // 2][:, (a % 2) * 256 + f * P:(a % 2) * 256 + (f + 1) * P]
                        nc.tensor.matmul(bank, AB[:, f, a, 0:P], BD[:, 0, :], start=True, stop=False)
                        mm = nc.tensor.matmul(bank, AB[:, f, a, P:2 * P], BD[:, 1, :], start=False, stop=True)
                    mm.then_inc(cd_full, 1)

                pe.wait_ge(fft_step, (l + 1) * FFT_STEPS)
                pe.wait_ge(tw_landed, (l + 1) * 16)
                for b in range(4):
                    pe.wait_ge(z_ev, l * 8 + b + 1)
                position_dft(0, 4)
                for b in range(4):
                    pe.wait_ge(z_ev, l * 8 + 4 + b + 1)
                position_dft(1, 0)
                project(2, lambda n, b: pe.wait_ge(ab_act if n < 4 else ab_dve, l * 4 + n % 4 + 1))

                pe.wait_ge(layer_landed, (l + 1) * (7 * 16))
                pe.wait_ge(ln_step, l * 10 + 10)
                for h in range(HB):
                    pe.wait_ge(q_ev, l * 8 + h + 1)
                    nc.tensor.matmul(B[4 + h][:, :].rearrange("p (n d) -> p n d", d=DH), WSP[:, h, :],
                                     UV[:, 1, :, h * DH:(h + 1) * DH], start=True, stop=True).then_inc(sp_full, 1)
                pe.wait_ge(q_ev, l * 8 + 8)
                pe.wait_ge(ab_dve, l * 4 + 4)
                channel_dft(0)
                channel_dft(1)
                project(3, lambda n, b: pe.wait_ge(mb_made if n < 4 else mc_made, l * 4 + n % 4 + 1))
                project(4, lambda n, b: pe.wait_ge(k_ev, l * 8 + n + 1))

                def scores(t):
                    j, rr, h = t // 16, (t // 8) % 2, t % 8
                    bank = B[t % 2][:, 0:NKEY]
                    if t >= 2:
                        pe.wait_ge(l_made, l * 64 + t - 1)
                    else:
                        pe.wait_ge(v_dve if t else v_act, l * 4 + 3)
                    hp = slice(DH * (h % 2), DH * (h % 2) + DH)
                    c = 3 * rr + COMBO[j]
                    mp = slice(32 * (c // 2), 32 * (c // 2) + 24)
                    nc.tensor.matmul(bank, ONEHOT[mp, :], MASK[mp, c % 2, :], start=True, stop=False)
                    q = QT[hp, h // 2, t // 8 * P:(t // 8 + 1) * P]
                    k = grid(KT[hp, h // 2, :])[:, 4 * rr:4 * rr + KR, BAND[j]:BAND[j] + KC]
                    nc.tensor.matmul(bank.rearrange("p (r c) -> p r c", c=KC), q, k,
                                     start=False, stop=True).then_inc(s_full, 1)

                def turn_probs(t):
                    pe.wait_ge(p_made, l * 64 + t + 1)
                    if t < 2:
                        pe.wait_ge(v_dve if t else v_act, l * 4 + 4)
                    if t >= 2:
                        pe.wait_ge(pt_made, l * 64 + t - 1)
                    for n in range(3):
                        mm = nc.tensor.transpose(B[2 + t % 2][:, n * P:(n + 1) * P], L[:, t % 3, n * P:(n + 1) * P],
                                                 IDENT[:, :])
                    mm.then_inc(pt_full, 1)

                def values(t):
                    j, rr, h = t // 16, (t // 8) % 2, t % 8
                    pe.wait_ge(pt_made, l * 64 + t + 1)
                    if t % 16 == 0:
                        pe.wait_ge(vb_landed[j % 2], l * (2 * 4 * 16) + (j // 2 + 1) * (4 * 16))
                    if h == 0 and t >= 16:
                        pe.wait_ge(o_made, l * 8 + t // 8 - 1)
                    cols = slice(h * DH, min(h + 2, HA) * DH)
                    for n in range(3):
                        mm = nc.tensor.matmul(B[4 + (t // 8) % 2][:, cols],
                                              PT[:, t % 2, n * P:(n + 1) * P],
                                              VB[j % 2][:, rr + n, cols],
                                              start=(n == 0), stop=(n == 2))
                    mm.then_inc(pv_done, 1)

                def turn_batch(b):
                    pe.wait_ge(hs_norm, l * 2 + b // 4 + 1)
                    if b >= 2:
                        pe.wait_ge(bt_lo, l * 8 + b - 1)
                    src = (MB, MC)[b // 4]
                    f, q = divmod(b % 4, 2)
                    for n in range(4):
                        mm = nc.tensor.transpose(B[6 + b % 2][:, n * P:(n + 1) * P],
                                                 src[:, 4 * q + n, f * P:(f + 1) * P], IDENT[:, :])
                    mm.then_inc(bt_full, 1)

                def out_product(g, n, b, stop):
                    s, k = ALL_SLOT[OUT_P + 4 * g + n // 2], OUT_ORDER[n]
                    m, h = slice((n % 2) * 512 + b // 2 * P, (n % 2) * 512 + (b // 2 + 1) * P), half(b % 2)
                    return split3(B[b][:, :], WH[s][:, m], WL[s][:, m], HH[:, k, h], HL[:, k, h], n == 0, stop)

                def out_early(b):
                    pe.wait_ge(*{0: (l_made, l * 64 + 64), 1: (l_made, l * 64 + 64), 2: (pt_made, l * 64 + 64),
                                 3: (pt_made, l * 64 + 64), 4: (o_made, l * 8 + 7), 5: (o_made, l * 8 + 8),
                                 6: (ot_lo, l * 32 + 28), 7: (ot_lo, l * 32 + 32)}[b])
                    for n in range(4):
                        mm = out_product(0, n, b, False)
                        if b == 7 and n % 2:
                            piece_done(OUT_P + n // 2, mm)

                pe.wait_ge(const_landed, 3 * 16)
                pe.wait_ge(mask_landed, (l + 1) * 16)
                for t in range(73):
                    if t == 67:
                        pe.wait_ge(bt_lo, l * 8 + 8)
                        wait_piece(OUT_P)
                        wait_piece(OUT_P + 1)
                        for b in range(3):
                            out_early(b)
                    if t < 64:
                        scores(t)
                    if 2 <= t <= 65:
                        turn_probs(t - 2)
                    if t < 8:
                        turn_batch(t)
                    if 3 <= t <= 66:
                        values(t - 3)
                    tile, ph = divmod(t - 9, 8)
                    if t >= 15 and ph == 6:
                        pe.wait_ge(o_norm, l * 8 + tile + 1)
                        for k in range(4):
                            mm = nc.tensor.transpose(B[6 + tile % 2][:, k * P:(k + 1) * P],
                                                     OT[:, 2 * k:2 * k + 2, :].rearrange("p h d -> p (h d)"),
                                                     IDENT[:, :])
                        mm.then_inc(ot_full, 1)

                for b in (3, 4, 6, 5, 7):
                    out_early(b)
                for g in range(2):
                    for n in range(0 if g else 4, KT_D):
                        p = OUT_P + 4 * g + n // 2
                        if n % 2 == 0:
                            wait_piece(p)
                        for b in range(8):
                            if n == 0:
                                pe.wait_ge(out_added, l * 16 + b + 1)
                            mm = out_product(g, n, b, n == KT_D - 1)
                            if n == KT_D - 1:
                                mm.then_inc(out_full, 1)
                        if n % 2:
                            piece_done(p, mm)

                def turn(i, first):
                    F = (l * NI + i) * 4
                    for f in range(2):
                        for h in range(2):
                            for g in range(2):
                                s = 2 * f + g
                                if h == 0:
                                    pe.wait_ge(w_ready[s], l * PER_SLOT[s] + i + (FFN_FIRST[s] + 1))
                                if first and f == 0:
                                    pe.wait_ge(out_added, l * 16 + 8 + 2 * g + h + 1)
                                pe.wait_ge(up_read if g else gate_read,
                                           F + (2 * f + h - 1 + (UP_CREDIT if g else GATE_CREDIT)))
                                for k in range(KT_D):
                                    if first and f == 0 and g == 0:
                                        pe.wait_ge(n_ffn.lo, l * 16 + FFN_LO.index((k, h)) + 1)
                                        if h == 1 and k == 5:
                                            pe.wait_ge(out_added, l * 16 + 16)
                                            sum_features(n_ffn, l, 0)
                                            sum_features(n_ffn, l, 1)
                                    m = slice(k * P, (k + 1) * P)
                                    mm = split3(B[2 * g + h][:, :], WH[s][:, m], WL[s][:, m],
                                                HH[:, at_k(k), half(h)], HL[:, at_k(k), half(h)],
                                                k == 0, k == KT_D - 1)
                                mm.then_inc(gu_full, 1)
                    for s in (4, 5):
                        pe.wait_ge(w_ready[s], l * PER_SLOT[s] + i + (FFN_FIRST[s] + 1))
                    for n in range(16):
                        h, k = divmod(n, 8)
                        if n in (0, 8):
                            pe.wait_ge(a_lo, F + (2 + h + 1 + SPLIT_CREDIT))
                        pe.wait_ge(dn_added, (l * NI + i) * 16 + (n - 3 + ADD_CREDIT))
                        m = slice(k * P, (k + 1) * P)
                        for f in range(2):
                            mm = split3(B[4 + n % 4][:, :], WH[4 + f][:, m], WL[4 + f][:, m],
                                        AH[:, f, half(h)], AL[:, f, half(h)], f == 0, f == 1)
                        mm.then_inc(dn_full, 1)

                turn(0, True)
                with pe.Fori(1, NI) as i:
                    turn(i, False)
            for h in range(2):
                if h == 0:
                    pe.wait_ge(dn_added, DEPTH * ADDS + ADD_CREDIT - 2)
                sum_features(n_fin, 0, h)


def constants():
    b = np.arange(P)[:, None, None]
    a = np.arange(8)[None, :, None]
    c = np.arange(P)[None, None, :]
    th = 2 * np.pi * (b * (a + 8 * c) % S) / S
    sign = np.where(np.arange(8) > 4, -1.0, 1.0)[None, :, None]
    tw = np.stack([np.concatenate([np.cos(th), -np.sin(th)], 2),
                   np.concatenate([np.sin(th), np.cos(th)], 2) * sign], 2)
    f = np.arange(P)
    same = f[:, None] // DH == f[None, :] // DH
    ph = 2 * np.pi * ((f[:, None] % DH) * (f[None, :] % DH) % DH) / DH
    scale = (S * DH) ** -0.5
    bd = np.stack([np.cos(ph) * same * scale, np.sin(ph) * same * scale], 1)
    onehot = np.zeros((3, 32, P), np.float32)
    qr, qc = np.divmod(np.arange(P), QC)
    onehot[:, qr, np.arange(P)] = NEG[1]
    onehot[:, 8 + qc, np.arange(P)] = NEG[1]
    mask = np.zeros((3, 32, 2, KR, KC), np.float32)
    for c in range(6):
        rr, j = c // 3, COMBO.index(c % 3)
        key = 4 * rr + np.arange(KR)
        for q in range(QR):
            first = min(max(QR * rr + q - KH // 2, 0), GROWS - KH)
            mask[c // 2, q, c % 2, (key < first) | (key >= first + KH), :] = NEG[0]
        key = BAND[j] + np.arange(KC)
        for q in range(QC):
            first = min(max(QC * j + q - KW // 2, 0), GW - KW)
            mask[c // 2, 8 + q, c % 2, :, (key < first) | (key >= first + KW)] = NEG[0]
    return dict(tw=tw.astype(np.float32), bd=bd.astype(np.float32), ident=np.eye(P, dtype=np.float32),
                onehot=onehot.reshape(96, P).astype(np.float16),
                mask=mask.reshape(96, 2, NKEY).astype(np.float16))


def features(g):
    return np.ascontiguousarray(np.swapaxes(g.reshape(g.shape[:-1] + (KT_D, P)), -1, -2))


def lay_out(x, norm_mix_g, w_in, rpb, gmlp_ln_g, gmlp_ln_b, w_spatial, b_spatial, head_norm_g, w_out,
            norm_ffn_g, w_gate, w_up, w_down, final_norm_g):
    ff = (DEPTH, KT_D, P, FT, P)
    pad = np.pad(rpb, ((0, 0), (0, 0), (4, 4), (16, 16)))
    qr, qc = np.divmod(np.arange(P), QC)
    rows = np.arange(BR)[None, :] - qr[:, None] + 7
    cols = np.arange(BC)[None, :] - qc[:, None] + 15
    bias = pad[:, :, rows[:, :, None], cols[:, None, :]]
    return dict(
        x=np.ascontiguousarray(x[0].T).reshape(KT_D, P, S),
        win=w_in.reshape(DEPTH, KT_D, P, IN_W), wout=w_out.reshape(DEPTH, KT_D, P, D),
        wg=np.ascontiguousarray(w_gate.reshape(ff).transpose(0, 3, 2, 1, 4)).reshape(DEPTH, FT, P, D),
        wu=np.ascontiguousarray(w_up.reshape(ff).transpose(0, 3, 2, 1, 4)).reshape(DEPTH, FT, P, D),
        wd=w_down.reshape(DEPTH, FT, P, D),
        bias=np.ascontiguousarray(bias.transpose(0, 2, 1, 3, 4)),
        wsp=np.ascontiguousarray(w_spatial.transpose(0, 3, 1, 2)),
        bsp=np.ascontiguousarray(b_spatial.transpose(0, 2, 1)),
        lng=np.ascontiguousarray(np.broadcast_to(gmlp_ln_g[:, None], (DEPTH, P, WB))),
        lnb=np.ascontiguousarray(np.broadcast_to(gmlp_ln_b[:, None], (DEPTH, P, WB))),
        gmix=features(norm_mix_g), ghead=features(head_norm_g), gffn=features(norm_ffn_g),
        gfin=features(final_norm_g), **constants())


def kernel(**inputs):
    import concourse.bacc as bacc
    from concourse.bass_utils import run_bass_kernel_spmd

    nc = bacc.Bacc("TRN2", target_bir_lowering=False, num_devices=1)
    arrays = lay_out(**{k: np.asarray(v) for k, v in inputs.items()})
    args = {n: nc.dram_tensor(f"in_{n}", a.shape, mybir.dt.from_np(a.dtype), kind="ExternalInput").ap()
            for n, a in arrays.items()}
    args["out"] = nc.dram_tensor("out_t_dram", (KT_D, P, S), F32, kind="ExternalOutput").ap()
    build(nc, **args)
    got = run_bass_kernel_spmd(nc, [{f"in_{n}": a for n, a in arrays.items()}], core_ids=[0])
    return np.ascontiguousarray(got.results[0]["out_t_dram"].reshape(D, S).T)[None]
```
